# Optimizing a Trainium2 kernel written in Bass

```python
import jax, jax.numpy as jnp
from jax import lax
import numpy as np
import math

D_MODEL = 1024
BATCH = 1
SEQ = 512
DEPTH = 2

RET_HEADS = 4
RET_DK = 128
RET_DV = 128
FOX_HEADS = 8
FOX_DH = 64
D_FF = 2816
CHUNK = 128
Q_BLOCK = 128
ROPE_BASE = 10000.0
EPS = 1e-6

RET_QK = RET_HEADS * RET_DK
RET_V = RET_HEADS * RET_DV
FOX_W = FOX_HEADS * FOX_DH
IN_SPLITS = (RET_QK, RET_QK, RET_V, RET_V, FOX_W, FOX_W, FOX_W, FOX_HEADS, D_MODEL, D_MODEL)
IN_COLS = sum(IN_SPLITS)


def rmsnorm(x, g):
    xf = x.astype(jnp.float32)
    y = xf * lax.rsqrt(jnp.mean(xf * xf, axis=-1, keepdims=True) + EPS)
    return (y * g.astype(jnp.float32)).astype(x.dtype)

def swiglu(h, w_in, w_out):
    gu = h @ w_in
    a, b = gu[..., :D_FF], gu[..., D_FF:]
    return (jax.nn.silu(a) * b) @ w_out

def split_cols(p):
    outs = []
    off = 0
    for w in IN_SPLITS:
        outs.append(p[..., off:off + w])
        off += w
    return outs

def to_heads(t, n_heads):
    b, s, _ = t.shape
    return t.reshape(b, s, n_heads, -1).transpose(0, 2, 1, 3)

def from_heads(t):
    b, h, s, d = t.shape
    return t.transpose(0, 2, 1, 3).reshape(b, s, h * d)

def rope(t):
    s, d = t.shape[2], t.shape[3]
    inv = jnp.power(ROPE_BASE, -jnp.arange(0, d, 2, dtype=jnp.float32) / d)
    ang = jnp.arange(s, dtype=jnp.float32)[:, None] * inv[None, :]
    cos, sin = jnp.cos(ang), jnp.sin(ang)
    tf = t.astype(jnp.float32)
    t1, t2 = tf[..., : d // 2], tf[..., d // 2:]
    return jnp.concatenate([t1 * cos - t2 * sin, t1 * sin + t2 * cos], axis=-1).astype(t.dtype)

def retention_chunkwise(q, k, v):
    in_dtype = v.dtype
    q = q.astype(jnp.float32)
    k = k.astype(jnp.float32) * (q.shape[-1] ** -0.5)
    v = v.astype(jnp.float32)
    b, h, s, dk = q.shape
    dv = v.shape[-1]
    n = s // CHUNK
    log_gamma = jnp.log1p(-jnp.exp2(-5.0 - jnp.arange(h, dtype=jnp.float32)))
    idx = jnp.arange(CHUNK, dtype=jnp.float32)
    diff = idx[:, None] - idx[None, :]
    decay_intra = jnp.where(diff >= 0, jnp.exp(log_gamma[:, None, None] * jnp.maximum(diff, 0.0)), 0.0)
    xi = jnp.exp(log_gamma[:, None] * (idx + 1.0))
    zeta = jnp.exp(log_gamma[:, None] * (CHUNK - 1.0 - idx))
    gamma_c = jnp.exp(log_gamma * CHUNK)

    qc = q.reshape(b, h, n, CHUNK, dk)
    kc = k.reshape(b, h, n, CHUNK, dk)
    vc = v.reshape(b, h, n, CHUNK, dv)

    scores = jnp.einsum('bhncd,bhnsd->bhncs', qc, kc) * decay_intra[None, :, None]
    inner = jnp.einsum('bhncs,bhnse->bhnce', scores, vc)

    kv = jnp.einsum('bhncd,bhnce->bhnde', kc * zeta[None, :, None, :, None], vc)

    def step(state, kv_n):
        return gamma_c[None, :, None, None] * state + kv_n, state

    _, state_prev = lax.scan(step, jnp.zeros((b, h, dk, dv), jnp.float32), jnp.moveaxis(kv, 2, 0))
    state_prev = jnp.moveaxis(state_prev, 0, 2)
    cross = jnp.einsum('bhncd,bhnde->bhnce', qc * xi[None, :, None, :, None], state_prev)
    return (inner + cross).reshape(b, h, s, dv).astype(in_dtype)

def forgetting_attention(q, k, v, log_f):
    b, h, s, d = q.shape
    c = jnp.cumsum(log_f, axis=-1)
    kpos = jnp.arange(s)
    scale = d ** -0.5
    n_blocks = s // Q_BLOCK

    def block(i):
        start = i * Q_BLOCK
        qb = lax.dynamic_slice_in_dim(q, start, Q_BLOCK, axis=2)
        cb = lax.dynamic_slice_in_dim(c, start, Q_BLOCK, axis=2)
        qpos = start + jnp.arange(Q_BLOCK)
        logits = jnp.einsum('bhqd,bhkd->bhqk', qb, k).astype(jnp.float32) * scale
        logits = logits + (cb[..., :, None] - c[..., None, :])
        logits = jnp.where(kpos[None, :] <= qpos[:, None], logits, -1e30)
        p = jax.nn.softmax(logits, axis=-1)
        return jnp.einsum('bhqk,bhkd->bhqd', p.astype(v.dtype), v)

    out = lax.map(block, jnp.arange(n_blocks))
    return jnp.moveaxis(out, 0, 2).reshape(b, h, s, d)

def mixing_sublayer(h, w_in, b_forget, ret_norm, w_o_ret, w_o_fox, w_out):
    proj = h @ w_in
    rq, rk, rv, rg, fq, fk, fv, ff, gate_r, gate_f = split_cols(proj)

    ret = retention_chunkwise(rope(to_heads(rq, RET_HEADS)), rope(to_heads(rk, RET_HEADS)), to_heads(rv, RET_HEADS))
    retf = ret.astype(jnp.float32)
    retf = retf * lax.rsqrt(jnp.mean(retf * retf, axis=-1, keepdims=True) + EPS)
    ret = from_heads(retf.astype(h.dtype)) * ret_norm
    y_ret = (jax.nn.silu(rg) * ret) @ w_o_ret

    log_f = jax.nn.log_sigmoid((ff + b_forget).astype(jnp.float32))
    fox = forgetting_attention(to_heads(fq, FOX_HEADS), to_heads(fk, FOX_HEADS), to_heads(fv, FOX_HEADS),
                               log_f.transpose(0, 2, 1))
    y_fox = from_heads(fox) @ w_o_fox

    merged = jax.nn.sigmoid(gate_r) * y_ret + jax.nn.sigmoid(gate_f) * y_fox
    return merged @ w_out

def first_inputs(seed: int = 0) -> dict:
    key = jax.random.key(seed)
    ks = jax.random.split(key, 16)
    f32 = jnp.float32

    def nrm(k, shape, fan_in):
        return jax.random.normal(k, shape, f32) * (fan_in ** -0.5)

    def gain(k, shape):
        return 1.0 + 0.02 * jax.random.normal(k, shape, f32)

    return {
        "x": jax.random.normal(ks[0], (BATCH, SEQ, D_MODEL), f32),
        "norm_ffn1": gain(ks[1], (DEPTH, D_MODEL)),
        "w_ffn1_in": nrm(ks[2], (DEPTH, D_MODEL, 2 * D_FF), D_MODEL),
        "w_ffn1_out": nrm(ks[3], (DEPTH, D_FF, D_MODEL), D_FF),
        "norm_mix": gain(ks[4], (DEPTH, D_MODEL)),
        "w_in": nrm(ks[5], (DEPTH, D_MODEL, IN_COLS), D_MODEL),
        "b_forget": jax.random.uniform(ks[6], (DEPTH, FOX_HEADS), f32, minval=1.0, maxval=4.0),
        "ret_norm": gain(ks[7], (DEPTH, RET_V)),
        "w_o_ret": nrm(ks[8], (DEPTH, RET_V, D_MODEL), RET_V),
        "w_o_fox": nrm(ks[9], (DEPTH, FOX_W, D_MODEL), FOX_W),
        "w_out": nrm(ks[10], (DEPTH, D_MODEL, D_MODEL), D_MODEL),
        "norm_ffn2": gain(ks[11], (DEPTH, D_MODEL)),
        "w_ffn2_in": nrm(ks[12], (DEPTH, D_MODEL, 2 * D_FF), D_MODEL),
        "w_ffn2_out": nrm(ks[13], (DEPTH, D_FF, D_MODEL), D_FF),
        "norm_final": gain(ks[14], (D_MODEL,)),
    }

def first_block(x, norm_ffn1, w_ffn1_in, w_ffn1_out, norm_mix, w_in, b_forget, ret_norm,
              w_o_ret, w_o_fox, w_out, norm_ffn2, w_ffn2_in, w_ffn2_out, norm_final):
    for l in range(DEPTH):
        x = x + 0.5 * swiglu(rmsnorm(x, norm_ffn1[l]), w_ffn1_in[l], w_ffn1_out[l])
        h = rmsnorm(x, norm_mix[l])
        x = x + mixing_sublayer(h, w_in[l], b_forget[l], ret_norm[l], w_o_ret[l], w_o_fox[l], w_out[l])
        x = x + 0.5 * swiglu(rmsnorm(x, norm_ffn2[l]), w_ffn2_in[l], w_ffn2_out[l])
    return rmsnorm(x, norm_final)


DEPTH_2 = 1

N_MEM = 256
MEM_HEADS = 4
MEM_HEAD_DIM = 128
MEM_WIDTH = MEM_HEADS * MEM_HEAD_DIM
D_RNN = 3 * D_MODEL // 4
LRU_BLOCK = 64
N_LRU_BLOCKS = D_RNN // LRU_BLOCK
CONV_WIDTH = 4
LRU_C = 8.0
DIL_GROUPS = ((128, 1), (512, 4), (2048, 16))
N_DIL_GROUPS = len(DIL_GROUPS)
HEADS_PER_GROUP = 4
DIL_HEAD_DIM = 64
N_DIL_HEADS = N_DIL_GROUPS * HEADS_PER_GROUP
DIL_QKV_WIDTH = 3 * N_DIL_HEADS * DIL_HEAD_DIM
DIL_OUT_WIDTH = HEADS_PER_GROUP * DIL_HEAD_DIM
NUM_BUCKETS = 32
MAX_DISTANCE = 2048
N_BRANCHES = 3
D_FF_2 = 4 * D_MODEL
NEG = -1e30

SPLITS = (D_RNN, 2 * D_RNN, 2 * D_RNN + DIL_QKV_WIDTH, 2 * D_RNN + DIL_QKV_WIDTH + MEM_WIDTH)
D_IN = 2 * D_RNN + DIL_QKV_WIDTH + MEM_WIDTH + N_BRANCHES * D_MODEL


def _rmsnorm(x, g):
    x32 = x.astype(jnp.float32)
    y = x32 * lax.rsqrt(jnp.mean(x32 * x32, axis=-1, keepdims=True) + EPS)
    return (y * g.astype(jnp.float32)).astype(x.dtype)

def _t5_bucket(dist):
    max_exact = NUM_BUCKETS // 2
    df = jnp.maximum(dist, 1).astype(jnp.float32)
    large = max_exact + (jnp.log(df / max_exact) / math.log(MAX_DISTANCE / max_exact)
                         * (NUM_BUCKETS - max_exact)).astype(jnp.int32)
    large = jnp.minimum(large, NUM_BUCKETS - 1)
    return jnp.where(dist < max_exact, dist, large)

def _rg_lru(xc, w_a, b_a, w_x, b_x, lam):
    B, S, C = xc.shape
    xb = xc.reshape(B, S, N_LRU_BLOCKS, LRU_BLOCK)
    r = jax.nn.sigmoid((jnp.einsum('bshi,hij->bshj', xb, w_a).reshape(B, S, C) + b_a).astype(jnp.float32))
    i = jax.nn.sigmoid((jnp.einsum('bshi,hij->bshj', xb, w_x).reshape(B, S, C) + b_x).astype(jnp.float32))
    log_a = -LRU_C * r * jax.nn.softplus(-lam.astype(jnp.float32))
    a = jnp.exp(log_a)
    mult = jnp.sqrt(-jnp.expm1(2.0 * log_a))
    b = mult * (i * xc.astype(jnp.float32))

    def combine(left, right):
        a1, b1 = left
        a2, b2 = right
        return a1 * a2, a2 * b1 + b2

    _, h = lax.associative_scan(combine, (a, b), axis=1)
    return h

def _dilated_group(q, k, v, table_g, dilation, span):
    B, S, H, Dh = q.shape
    L = S // dilation
    nb = -(-L // span)
    Lp = nb * span

    def to_blocks(t):
        t = t.reshape(B, L, dilation, H, Dh).transpose(0, 2, 3, 1, 4)
        t = jnp.pad(t, ((0, 0), (0, 0), (0, 0), (0, Lp - L), (0, 0)))
        return t.reshape(B, dilation, H, nb, span, Dh)

    def with_prev(t):
        prev = jnp.pad(t, ((0, 0), (0, 0), (0, 0), (1, 0), (0, 0), (0, 0)))[:, :, :, :-1]
        return jnp.concatenate([prev, t], axis=-2)

    qb = to_blocks(q)
    kk = with_prev(to_blocks(k))
    vv = with_prev(to_blocks(v))

    qi = jnp.arange(span)[:, None]
    kj = jnp.arange(2 * span)[None, :]
    off = qi + span - kj
    valid = (off >= 0) & (off <= span)
    mask = valid[None] & ((jnp.arange(nb)[:, None, None] > 0) | (kj >= span)[None])
    bucket = _t5_bucket(jnp.maximum(off, 0) * dilation)
    bias = jnp.transpose(table_g.astype(jnp.float32)[bucket], (2, 0, 1))

    s = jnp.einsum('brhnqc,brhnkc->brhnqk', qb, kk) * (DIL_HEAD_DIM ** -0.5) + bias[None, None, :, None]
    s = jnp.where(mask[None, None, None], s, NEG)
    m = jnp.max(s, axis=-1, keepdims=True)
    p = jnp.exp(s - m)
    den = jnp.sum(p, axis=-1)
    o = jnp.einsum('brhnqk,brhnkc->brhnqc', p, vv) / den[..., None]
    lse = m[..., 0] + jnp.log(den)

    o = o.reshape(B, dilation, H, Lp, Dh)[:, :, :, :L].transpose(0, 3, 1, 2, 4).reshape(B, S, H, Dh)
    lse = lse.reshape(B, dilation, H, Lp)[:, :, :, :L].transpose(0, 3, 1, 2).reshape(B, S, H)
    return o, lse

def second_inputs(seed: int = 0) -> dict:
    key = jax.random.key(seed)
    ks = jax.random.split(key, 24)
    f32 = jnp.float32

    def nrm(k, shape, fan_in):
        return jax.random.normal(k, shape, f32) * (fan_in ** -0.5)

    def gain(k, n):
        return 1.0 + 0.05 * jax.random.normal(k, (n,), f32)

    u = jax.random.uniform(ks[11], (D_RNN,), f32, 0.9, 0.999)
    sig = u ** (1.0 / LRU_C)
    lam = jnp.log(sig) - jnp.log1p(-sig)
    return {
        "x": jax.random.normal(ks[0], (BATCH, SEQ, D_MODEL), f32),
        "mem": jax.random.normal(ks[1], (BATCH, N_MEM, D_MODEL), f32),
        "g_mix": gain(ks[2], D_MODEL),
        "w_in": nrm(ks[3], (D_MODEL, D_IN), D_MODEL),
        "b_gate": 0.01 * jax.random.normal(ks[4], (N_BRANCHES * D_MODEL,), f32),
        "conv_w": nrm(ks[5], (CONV_WIDTH, D_RNN), CONV_WIDTH),
        "conv_b": 0.01 * jax.random.normal(ks[6], (D_RNN,), f32),
        "w_rg_a": nrm(ks[7], (N_LRU_BLOCKS, LRU_BLOCK, LRU_BLOCK), LRU_BLOCK),
        "b_rg_a": 0.01 * jax.random.normal(ks[8], (D_RNN,), f32),
        "w_rg_x": nrm(ks[9], (N_LRU_BLOCKS, LRU_BLOCK, LRU_BLOCK), LRU_BLOCK),
        "b_rg_x": 0.01 * jax.random.normal(ks[10], (D_RNN,), f32),
        "lru_lambda": lam,
        "w_lru_out": nrm(ks[12], (D_RNN, D_MODEL), D_RNN),
        "rel_bias": 0.1 * jax.random.normal(ks[13], (NUM_BUCKETS, N_DIL_HEADS), f32),
        "w_dil_out": nrm(ks[14], (DIL_OUT_WIDTH, D_MODEL), DIL_OUT_WIDTH),
        "g_mem": gain(ks[15], D_MODEL),
        "w_mem_kv": nrm(ks[16], (D_MODEL, 2 * MEM_WIDTH), D_MODEL),
        "w_mem_out": nrm(ks[17], (MEM_WIDTH, D_MODEL), MEM_WIDTH),
        "w_out": nrm(ks[18], (D_MODEL, D_MODEL), D_MODEL),
        "g_mlp": gain(ks[19], D_MODEL),
        "w_mlp_in": nrm(ks[20], (D_MODEL, D_FF_2), D_MODEL),
        "w_mlp_out": nrm(ks[21], (D_FF_2, D_MODEL), D_FF_2),
        "g_final": gain(ks[22], D_MODEL),
    }

def second_block(x, mem, g_mix, w_in, b_gate, conv_w, conv_b, w_rg_a, b_rg_a, w_rg_x, b_rg_x,
              lru_lambda, w_lru_out, rel_bias, w_dil_out, g_mem, w_mem_kv, w_mem_out, w_out,
              g_mlp, w_mlp_in, w_mlp_out, g_final):
    B, S, D = x.shape
    dt = x.dtype
    f32 = jnp.float32
    mem_n = _rmsnorm(mem, g_mem)

    for _ in range(DEPTH_2):
        h = _rmsnorm(x, g_mix)
        proj = h @ w_in
        x_lru, gate_lru, qkv, q_mem, gates = jnp.split(proj, SPLITS, axis=-1)

        xc = lax.conv_general_dilated(x_lru, conv_w[:, None, :].astype(x_lru.dtype), window_strides=(1,),
                                      padding=[(CONV_WIDTH - 1, 0)], dimension_numbers=('NWC', 'WIO', 'NWC'),
                                      feature_group_count=D_RNN) + conv_b
        hl = _rg_lru(xc, w_rg_a, b_rg_a, w_rg_x, b_rg_x, lru_lambda)
        y_lru = (jax.nn.gelu(gate_lru.astype(f32)) * hl).astype(dt) @ w_lru_out

        qkv = qkv.astype(f32).reshape(B, S, 3, N_DIL_GROUPS, HEADS_PER_GROUP, DIL_HEAD_DIM)
        outs, lses = [], []
        for g, (window, dil) in enumerate(DIL_GROUPS):
            o_g, lse_g = _dilated_group(qkv[:, :, 0, g], qkv[:, :, 1, g], qkv[:, :, 2, g],
                                        rel_bias[:, g * HEADS_PER_GROUP:(g + 1) * HEADS_PER_GROUP],
                                        dil, window // dil)
            outs.append(o_g)
            lses.append(lse_g)
        alpha = jax.nn.softmax(jnp.stack(lses, axis=0), axis=0)
        o_dil = jnp.sum(alpha[..., None] * jnp.stack(outs, axis=0), axis=0)
        y_dil = o_dil.reshape(B, S, DIL_OUT_WIDTH).astype(dt) @ w_dil_out

        kv = (mem_n @ w_mem_kv).astype(f32).reshape(B, N_MEM, 2, MEM_HEADS, MEM_HEAD_DIM)
        qm = q_mem.astype(f32).reshape(B, S, MEM_HEADS, MEM_HEAD_DIM)
        sm = jnp.einsum('bqhc,bkhc->bhqk', qm, kv[:, :, 0]) * (MEM_HEAD_DIM ** -0.5)
        pm = jax.nn.softmax(sm, axis=-1)
        om = jnp.einsum('bhqk,bkhc->bqhc', pm, kv[:, :, 1]).reshape(B, S, MEM_WIDTH)
        y_mem = om.astype(dt) @ w_mem_out

        gt = jax.nn.sigmoid((gates + b_gate).astype(f32)).reshape(B, S, N_BRANCHES, D)
        merged = (gt[:, :, 0] * y_lru.astype(f32) + gt[:, :, 1] * y_dil.astype(f32)
                  + gt[:, :, 2] * y_mem.astype(f32)).astype(dt)
        x = x + merged @ w_out

        hm = _rmsnorm(x, g_mlp)
        x = x + jnp.square(jax.nn.relu(hm @ w_mlp_in)) @ w_mlp_out

    return _rmsnorm(x, g_final)


def setup_inputs(seed=0):
    out = dict(first_inputs(seed))
    for name, value in second_inputs(seed + 1).items():
        if name != "x":
            out[name + "_2"] = value
    return out


def reference(
    x, norm_ffn1, w_ffn1_in, w_ffn1_out, norm_mix, w_in, b_forget, ret_norm, w_o_ret, w_o_fox,
    w_out, norm_ffn2, w_ffn2_in, w_ffn2_out, norm_final, mem_2, g_mix_2, w_in_2, b_gate_2,
    conv_w_2, conv_b_2, w_rg_a_2, b_rg_a_2, w_rg_x_2, b_rg_x_2, lru_lambda_2, w_lru_out_2,
    rel_bias_2, w_dil_out_2, g_mem_2, w_mem_kv_2, w_mem_out_2, w_out_2, g_mlp_2, w_mlp_in_2,
    w_mlp_out_2, g_final_2,
):
    x = first_block(
        x, norm_ffn1, w_ffn1_in, w_ffn1_out, norm_mix, w_in, b_forget, ret_norm, w_o_ret,
        w_o_fox, w_out, norm_ffn2, w_ffn2_in, w_ffn2_out, norm_final,
    )
    return second_block(
        x, mem_2, g_mix_2, w_in_2, b_gate_2, conv_w_2, conv_b_2, w_rg_a_2, b_rg_a_2, w_rg_x_2,
        b_rg_x_2, lru_lambda_2, w_lru_out_2, rel_bias_2, w_dil_out_2, g_mem_2, w_mem_kv_2,
        w_mem_out_2, w_out_2, g_mlp_2, w_mlp_in_2, w_mlp_out_2, g_final_2,
    )


_drawn_inputs = setup_inputs


def setup_inputs(seed=0):
    import zlib

    import numpy as np

    out = dict(_drawn_inputs(seed))
    spreads = {}
    factors = {'norm_ffn1': 3.401,
     'ret_norm': 5.739,
     'norm_ffn2': 4.637,
     'g_mix_2': 2.947,
     'b_gate_2': 23.994,
     'conv_b_2': 3.352,
     'b_rg_a_2': 64.0,
     'b_rg_x_2': 57.054,
     'rel_bias_2': 7.714,
     'g_mem_2': 8.0,
     'g_mlp_2': 4.292}
    for name, (base, spread) in spreads.items():
        noise = np.random.default_rng([zlib.crc32(name.encode()), seed]).standard_normal(out[name].shape)
        drawn = base * np.exp(spread * noise) if base else spread * noise
        out[name] = __import__('jax').numpy.asarray(drawn.astype(out[name].dtype))
    for name, factor in factors.items():
        out[name] = (out[name] * factor).astype(out[name].dtype)
    return out
```

```python
from collections import deque
from contextlib import ExitStack

import numpy as np
import concourse.bass as bass
from concourse import mybir

P = 128
S = 512
TT = S // P
D = 1024
DT = D // P
EPS = 1e-6
NEG = -1e30
LOWEST = -3.0e38
DEPTH = 2
FF = 2816
RH = 4
FH, FDH = 8, 64
NMEM = 256
MH = 4
RNN = 768
RT = RNN // P
GH, GD = 4, 64
NB = 32
FF2 = 4096
DIL = 4

UNIT = 1024
RAW, SPLIT, AHEAD = 3, 3, 2

F32, F32R, I32 = mybir.dt.float32, mybir.dt.float32r, mybir.dt.int32
ALU, ACT = mybir.AluOpType, mybir.ActivationFunctionType
AX = mybir.AxisListType

VEC = {}


def _vec_layout():
    at = 0
    for name, n in (("norm_ffn1", 2 * DT), ("norm_mix", 2 * DT), ("norm_ffn2", 2 * DT), ("norm_final", DT),
                    ("ret_norm", 2 * RH), ("b_forget", 2), ("g_mix_2", DT), ("b_gate_2", 3 * DT),
                    ("conv_w_2", 4 * RT), ("conv_b_2", RT), ("b_rg_a_2", RT), ("b_rg_x_2", RT),
                    ("lru_lambda_2", RT), ("g_mem_2", DT), ("g_mlp_2", DT), ("g_final_2", DT)):
        VEC[name] = (at, n)
        at += n
    return at


NVEC = _vec_layout()


def unit_blocks(n_k, tiles):
    step = UNIT // (P * tiles)
    return [(k, min(step, n_k - k)) for k in range(0, n_k, step)]


def ffn_pieces(n_hidden):
    half = (n_hidden // 2 + 1) // 2 * 2
    return [(0, half), (half, n_hidden - half)]


def swiglu_groups(first, count):
    out = []
    for j in range(first, first + count, 2):
        out += [[j, j + 1], [FF // P + j, FF // P + j + 1]]
    return out


def pairs(first, count):
    return [[j, j + 1] for j in range(first, first + count, 2)]


class Step:

    def __init__(self, lane, fn, after, sem, by):
        self.lane, self.fn, self.after, self.sem, self.by = lane, fn, after, sem, by
        self.used, self.value = False, None


def flat(x):
    if x is None:
        return
    if isinstance(x, (list, tuple)):
        for y in x:
            yield from flat(y)
    else:
        yield x


class Lane:

    def __init__(self, sem):
        self.sem, self.items = sem, []

    def do(self, fn, after=(), place=None, sem=None, by=1):
        after = list(flat(after))
        for s in after:
            s.used = True
        step = Step(self, fn, after, self.sem if sem is None else sem, by)
        (self.items if place is None else place).append(step)
        return step

    def place(self):
        self.items.append([])
        return self.items[-1]

    def steps(self):
        return list(flat(self.items))


def count(lanes):
    totals = {}
    for lane in lanes:
        for s in lane.steps():
            if s.used or s.by == 16:
                totals[id(s.sem)] = totals.get(id(s.sem), 0) + s.by
                s.value = totals[id(s.sem)]


def emit(lane, eng):
    seen = {}
    for s in lane.steps():
        need = {}
        for a in s.after:
            k = id(a.sem)
            if a.value > seen.get(k, 0) and a.value > need.get(k, (None, 0))[1]:
                need[k] = (a.sem, a.value)
        for k, (sem, value) in need.items():
            eng.wait_ge(sem, value)
            seen[k] = value
        ins = s.fn(eng)
        if s.value is not None:
            ins.then_inc(s.sem, s.by)


class Buf:

    def __init__(self, ap):
        self.ap, self.free, self.ready = ap, [], []


class Ring:
    def __init__(self, bufs):
        self.bufs, self.n = bufs, 0

    def take(self):
        self.n += 1
        return self.bufs[(self.n - 1) % len(self.bufs)]


class Pair:

    def __init__(self, hi, lo):
        self.hi, self.lo, self.ready, self.used = hi, lo, {}, []


def tiles(t):
    return [t[:, j, :] for j in range(t.shape[1])]


def build(nc, x_in, vec_in, ident_in, tri_in, decay_in, rope_in, sel_in, mem_in, onehot_in, band_in, table_in,
          rg_in, w, out):
    ctx = ExitStack()
    with ctx:
        def sb(name, shape, dt=F32):
            return ctx.enter_context(nc.sbuf_tensor(name, shape, dt))

        def overlay(*plans):
            out, most = {}, 0
            for plan in plans:
                size = 0
                with ExitStack() as inner:
                    for name, shape, dt in plan:
                        out[name] = inner.enter_context(nc.sbuf_tensor(name, shape, dt))
                        size += int(np.prod(shape[1:]))
                most = max(most, size)
            ctx.enter_context(nc.sbuf_tensor("overlay_room", [P, most], F32))
            return out

        def sem(name):
            return ctx.enter_context(nc.semaphore(name))

        pe, act, dve, pool, sp = lanes = [Lane(sem(n)) for n in
                                          ("pe_done", "act_done", "dve_done", "pool_done", "sp_done")]
        raw_sem = [sem(f"unit_loaded_{i}") for i in range(RAW)]
        const_sem, bias_sem, out_sem = sem("constants_loaded"), sem("bias_moved"), sem("output_stored")
        rg_sem = [sem(f"recurrence_weights_loaded_{i}") for i in range(2)]
        tile_sem = [sem(f"bias_tile_loaded_{i}") for i in range(2)]


        xT_sb = sb("xT", [P, DT, S])
        in_hi, in_lo = sb("in_hi", [P, DT, S], F32R), sb("in_lo", [P, DT, S], F32R)
        raw = sb("raw", [P, RAW, UNIT])
        w_hi, w_lo = sb("w_hi", [P, SPLIT, UNIT], F32R), sb("w_lo", [P, SPLIT, UNIT], F32R)
        vec = sb("vec", [P, NVEC])
        ident, ones, tri = sb("ident", [P, P]), sb("ones", [P, P]), sb("tri", [P, P])
        rstd_sb, ssum_sb = sb("rstd_b", [P, S]), sb("ssum", [P, S])
        stat_sb = sb("stat", [P, 8, 8])
        soft_sb = sb("soft", [P, 4, 4])
        col_sb = sb("col", [P, 3, 8])
        lruv = sb("lruv", [P, 10, RT])
        table_sb = sb("rel_table", [P, 3 * GH])
        halfb = sb("halfb", [P, 3 * DT])
        NTMP = 5
        tmp_sb = sb("tmp", [P, NTMP, S])

        HID = 16
        f, r = F32, F32R
        m = overlay(
            [("hid_hi", [P, HID, S], r), ("hid_lo", [P, HID, S], r), ("silu", [P, 4, S], f)],
            [("gap_0", [P, 32, S], f), ("onehot", [P, 3, 2 * S], f), ("rel", [P, 3, 2 * S], f)],
            [("fq", [P, 4, S], f), ("fk", [P, 4, S], f), ("rq", [P, RH, S], f), ("rk", [P, RH, S], f),
             ("fv", [P, TT, S], f), ("rv", [P, TT, S], f), ("gate", [P, 2 * DT, S], f),
             ("srg", [P, RH, S], f), ("decay", [P, RH, S], f), ("p_1", [P, 2, S], f),
             ("pt_1", [P, 2, S], f), ("negc", [P, S], f)],
            [("fox_hi", [P, 4, S], r), ("fox_lo", [P, 4, S], r), ("ret_hi", [P, RH, S], r),
             ("ret_lo", [P, RH, S], r), ("gap_1", [P, 16, S], f), ("sel", [P, FH * P], f),
             ("rope", [P, 4, S], f)],
            [("dq", [P, 6, S], f), ("dk", [P, 6, S], f), ("lru_hi", [P, RT, S], r),
             ("lru_lo", [P, RT, S], r), ("mq", [P, MH, S], f), ("dv", [P, TT, 3, GH * GD], f),
             ("mk", [P, MH, NMEM], f), ("mv", [P, 2, MH * P], f), ("p_2", [P, 2, 768], f),
             ("pt_2", [P, 768], f), ("bias", [P, 2, 768], f), ("dil_hi", [P, 2, S], r),
             ("dil_lo", [P, 2, S], r), ("pad", [P, S + 4], f), ("rgw", [P, 2, 2 * P], f)],
            [("gap_7", [P, 12, S], f), ("lru_x", [P, RT, S], f), ("lru_g", [P, RT, S], f)],
            [("acc", [P, DT, S], f), ("memo_lo", [P, MH, S], r), ("gate2", [P, DT, S], f),
             ("mrg2_hi", [P, DT, S], r), ("memo_hi", [P, MH, S], r), ("mrg2_lo", [P, DT, S], r)],
            [("gap_5", [P, 16, S], f), ("mrg_hi", [P, DT, S], r), ("gap_6", [P, 16, S], f),
             ("mrg_lo_a", [P, 4, S], r), ("gap_8", [P, 4, S], f), ("mrg_lo_b", [P, 4, S], r)],
            [("gap_4", [P, 38, S], f), ("mem_hi", [P, DT, NMEM], r), ("mem_lo", [P, DT, NMEM], r),
             ("memx", [P, DT, NMEM], f), ("mem_rstd", [P, NMEM], f), ("mem_ssum", [P, NMEM], f)])

        bank = [Buf(ctx.enter_context(nc.psum_tensor(f"bank_{i}", [P, S], F32))[:]) for i in range(4)]
        score_ps = ctx.enter_context(nc.psum_tensor("score_ps", [P, 2 * S], F32))
        score = [Buf(score_ps[:, i * S:(i + 1) * S]) for i in range(2)]
        turn = Buf(ctx.enter_context(nc.psum_tensor("turn_ps", [P, S], F32))[:])
        outp = Buf(ctx.enter_context(nc.psum_tensor("out_ps", [P, S], F32))[:])

        def load(dst, src, sem, after=(), place=None):
            return sp.do(lambda e: e.dma_start(dst, src), after, place=place, sem=sem, by=16)

        const_loads = [load(d[:], a, const_sem) for d, a in ((xT_sb, x_in), (vec, vec_in), (ident, ident_in), (tri, tri_in))]
        x_loaded = const_loads[-1]
        first_loads = list(const_loads)
        ones_set = dve.do(lambda e: e.memset(ones[:], 1.0))

        def col(name, j, rows=P):
            return vec[0:rows, VEC[name][0] + j:VEC[name][0] + j + 1]

        tmp = Ring([Buf(tmp_sb[:, i, :]) for i in range(NTMP)])
        xT = [Buf(xT_sb[:, j, :]) for j in range(DT)]
        for j in range(DT):
            xT[j].ready = [x_loaded]

        class Units:
            n = 0
            places, load_places = [], []
            hi, lo, used = [], [], []
            cursor = {name: 0 for name in w}

        def next_unit(name, cols):
            i = Units.n
            Units.n += 1
            rs, ss = i % RAW, i % SPLIT
            at = Units.cursor[name]
            Units.cursor[name] += P * cols
            src = w[name][at:at + P * cols].rearrange("(p n) -> p n", p=P)
            loaded = load(raw[:, rs, 0:cols], src, raw_sem[rs],
                          [Units.hi[i - RAW], Units.lo[i - RAW]] if i >= RAW else [], place=Units.load_places[i])
            freed = [Units.used[i - SPLIT]] if i >= SPLIT else []
            a_place, d_place = Units.places[i]
            wr, wh, wl = raw[:, rs, 0:cols], w_hi[:, ss, 0:cols], w_lo[:, ss, 0:cols]
            hi = act.do(lambda e: e.activation(wh, wr, ACT.Copy), [loaded, freed], place=a_place)
            lo = dve.do(lambda e: e.tensor_tensor(wl, wr, wh.bitcast(F32), ALU.subtract),
                        [loaded, hi, freed], place=d_place)
            Units.hi.append(hi)
            Units.lo.append(lo)
            return wh, wl, [hi, lo]

        filler = deque()
        hooks = deque()
        rate = [1]
        waiting = []

        put = [None]
        soon = []

        def put_off(fn):
            if put[0] is None:
                fn()
            else:
                put[0].append(fn)

        def run_soon():
            now, soon[:] = list(soon), []
            for fn in now:
                fn()

        def drain():
            while filler:
                filler.popleft()()

        def flush():
            run_soon()
            while waiting:
                waiting.pop(0)()

        class Groups:
            n = 0

        def gemm(name, n_k, groups, src, evict, first_k=0, n=S, rows=None):
            for group in groups:
                banks = [bank[2 * (Groups.n % 2) + i] for i in range(2)]
                Groups.n += 1
                nt = len(group)
                if rows is None:
                    outs = [(banks[m], banks[m].ap[:, 0:n]) for m in range(nt)]
                else:
                    outs = [(banks[t // 2], banks[t // 2].ap[:, (t % 2) * 256:(t % 2) * 256 + 256])
                            for t in range(len(rows))]
                done = [None] * len(outs)
                for k0, nk in unit_blocks(n_k, nt):
                    wh, wl, w_ready = next_unit(name, nk * nt * P)
                    if any(first_k + k0 + k not in src.ready for k in range(nk)):
                        flush()
                    wh3 = wh.rearrange("p (k c) -> p k c", k=nk)
                    wl3 = wl.rearrange("p (k c) -> p k c", k=nk)
                    pops, at, total = 0, 0, len(outs) * nk
                    for o, (b, ps) in enumerate(outs):
                        for k in range(nk):
                            kk = first_k + k0 + k
                            after = [src.ready[kk], w_ready, b.free if k0 + k == 0 else []]
                            first = k0 + k == 0 and (rows is None or o % 2 == 0)
                            last = k0 + k == n_k - 1
                            for step, (xa, wa) in enumerate(((src.hi, wh3), (src.lo, wh3), (src.hi, wl3))):
                                if rows is None:
                                    lhs, rhs = wa[:, k, o * P:(o + 1) * P], xa[kk]
                                else:
                                    lhs, rhs = rows[o](xa[kk]), wa[:, k, :]
                                done[o] = pe.do(
                                    lambda e, ps=ps, lhs=lhs, rhs=rhs, st=first and step == 0, sp_=last and step == 2:
                                    e.matmul(ps, lhs, rhs, start=st, stop=sp_, skip_group_check=True),
                                    after if step == 0 else [])
                            at += 1
                            while pops < rate[0] and at < total and at >= (pops + 1) * total // (rate[0] + 1):
                                pops += 1
                                if filler:
                                    filler.popleft()()
                    Units.used.append(done[-1])
                    src.used = [done[-1]]
                    Units.places.append((act.place(), dve.place()))
                    Units.load_places.append(sp.place())
                    if hooks:
                        hooks.popleft()()
                    flush()

                def evict_group(group=group, outs=outs, done=list(done), banks=banks):
                    frees = {id(b): [] for b in banks}
                    put[0] = late = []
                    for o, (b, ps) in enumerate(outs):
                        frees[id(b)].append(evict(group[o] if rows is None else (group, o), ps, done[o if rows is None else -1]))
                    for b in banks:
                        b.free = frees[id(b)]
                    put[0] = None
                    for fn in late:
                        fn()

                waiting.append(evict_group)

        def split(x_ap, x_ready, dst, j, scale=None):
            hi_ap, lo_ap = dst.hi[j], dst.lo[j]
            used = list(flat(dst.used))
            if scale is None:
                hi = act.do(lambda e: e.activation(hi_ap, x_ap, ACT.Copy), [x_ready, used])
            else:
                hi = act.do(lambda e: e.activation(hi_ap, x_ap, ACT.Copy, scale=scale), [x_ready, used])
            steps = [hi]

            def low():
                if scale is None:
                    lo = dve.do(lambda e: e.tensor_tensor(lo_ap, x_ap, hi_ap.bitcast(F32), ALU.subtract),
                                [x_ready, hi, used])
                else:
                    lo = dve.do(lambda e: e.scalar_tensor_tensor(lo_ap, x_ap, scale, hi_ap.bitcast(F32),
                                                                 ALU.mult, ALU.subtract), [x_ready, hi, used])
                steps.append(lo)
                dst.ready[j] = steps
            put_off(low)
            return steps

        inp = Pair(tiles(in_hi), tiles(in_lo))

        def square_sum(x_ap, ready, j, ssum):
            if j == 0:
                ssum.ready = [act.do(lambda e: e.activation(ssum.ap, x_ap, ACT.Square), [ready, ssum.free])]
                return ssum.ready
            t = tmp.take()
            n = ssum.ap.shape[1]
            sq = act.do(lambda e: e.activation(t.ap[:, 0:n], x_ap, ACT.Square), [ready, t.free])
            add = pool.do(lambda e: e.tensor_tensor(ssum.ap, ssum.ap, t.ap[:, 0:n], ALU.add), [sq, ssum.ready])
            t.free, ssum.ready = [add], [add]
            return [sq]

        def norm_tile(j, gain, ssum, gain_at=0):
            if j == 0:
                inp.ready = {}
            x = xT[j]
            x.free = [split(x.ap, x.ready, inp, j, scale=col(gain, gain_at + j)), square_sum(x.ap, x.ready, j, ssum)]

        stat_free = [[]]

        def rsqrt(v_ap, ready, n, over, dst):
            c = [stat_sb[:, i, 0:n] for i in range(8)]
            last = dve.do(lambda e: e.tensor_scalar(c[0], v_ap, 1.0 / over, EPS, ALU.mult, ALU.add),
                          [ready, stat_free[0]])
            read = last
            last = dve.do(lambda e: e.tensor_scalar(c[1].bitcast(I32), c[0].bitcast(I32), 1, None,
                                                    ALU.logical_shift_right), last)
            last = dve.do(lambda e: e.tensor_scalar(c[2].bitcast(I32), c[1].bitcast(I32), -1, 0x5F3759DF,
                                                    ALU.mult, ALU.add), last)
            y = 2
            for it in range(4):
                z = 5 if y == 2 else 2
                to = dst.ap[:, 0:n] if it == 3 else c[z]
                last = dve.do(lambda e, y=y: e.tensor_tensor(c[3], c[y], c[y], ALU.mult), last)
                last = dve.do(lambda e: e.scalar_tensor_tensor(c[4], c[3], -0.5, c[0], ALU.mult, ALU.mult), last)
                last = dve.do(lambda e, y=y, to=to: e.scalar_tensor_tensor(to, c[4], 1.5, c[y], ALU.add, ALU.mult),
                              [last, dst.free if it == 3 else []])
                y = z
            dst.ready = [last]
            stat_free[0] = [last]
            return read

        tok_tiles = [lambda ap, t=t: ap[:, t * P:(t + 1) * P] for t in range(TT)]
        res_tiles = [lambda ap, r=r: ap[:, r::DIL] for r in range(DIL)]

        def stats(ssum, dst, tok, over=D):
            for i, tile in enumerate(tok):
                got = pe.do(lambda e, i=i, tile=tile: e.matmul(turn.ap[:, i:i + 1], tile(ssum.ap), ones[:, 0:1],
                                                               start=True, stop=True, skip_group_check=True),
                            [ssum.ready, ones_set, turn.free])
            ssum.free = [got]
            turn.free = [rsqrt(turn.ap[:, 0:len(tok)], got, len(tok), over, dst)]

        def spread(cols, dst, half=False):
            n = dst.ap.shape[1]
            t = tmp.take()
            for i in range(n // P):
                dg = dve.do(lambda e, i=i: e.tensor_scalar(t.ap[:, i * P:(i + 1) * P], ident[:],
                                                           cols.ap[:, i:i + 1], 0.5 if half else 1.0,
                                                           ALU.mult, ALU.mult),
                            [cols.ready, t.free, first_loads])
            for i in range(n // P):
                got = pe.do(lambda e, i=i: e.matmul(turn.ap[:, i * P:(i + 1) * P], ones[:],
                                                    t.ap[:, i * P:(i + 1) * P], start=True, stop=True,
                                                    skip_group_check=True),
                            [dg, turn.free])
            t.free = [got]
            copied = act.do(lambda e: e.activation(dst.ap, turn.ap[:, 0:n], ACT.Copy), [got, dst.free])
            turn.free = [copied]
            dst.ready, cols.free = [copied], [dg]

        ssum, rstd = Buf(ssum_sb[:]), Buf(rstd_sb[:])
        rcol, hcol, mcol = [Buf(col_sb[:, i, :]) for i in range(3)]

        def norm_hooks(ssum_, cols, dst, tok=tok_tiles, over=D):
            hooks.extend([lambda: None, lambda: stats(ssum_, cols, tok, over),
                          lambda: spread(cols, dst)])

        def times_rstd(dst_ap, ps, done, free=()):
            step = dve.do(lambda e: e.tensor_tensor(dst_ap, ps, rstd.ap, ALU.mult), [done, rstd.ready, free])
            rstd.free = [step]
            return step

        def add_residual(j, ps, done, scale):
            x = xT[j]
            step = dve.do(lambda e: e.scalar_tensor_tensor(x.ap, ps, scale, x.ap, ALU.mult, ALU.add),
                          [done, x.ready, x.free])
            x.ready, x.free = [step], []
            return step

        hid = Pair(tiles(m["hid_hi"]), tiles(m["hid_lo"]))
        silu = Ring([Buf(t) for t in tiles(m["silu"])])

        def feed_forward(w_in, w_out, n_hidden, gated, scale, after_tile):
            for first, n in ffn_pieces(n_hidden):
                held = {}

                def evict_gated(tile, ps, done, first=first, held=held):
                    if tile < n_hidden:
                        b = silu.take()
                        a = times_rstd(b.ap, ps, done, b.free)
                        b.ready = [act.do(lambda e: e.activation(b.ap, b.ap, ACT.Silu), a)]
                        held[tile] = b
                        return a
                    b = held[tile - n_hidden]
                    t = tmp.take()
                    up = times_rstd(t.ap, ps, done, t.free)
                    g = dve.do(lambda e: e.tensor_tensor(t.ap, t.ap, b.ap, ALU.mult), [up, b.ready])
                    b.free = [g]
                    t.free = split(t.ap, g, hid, tile - n_hidden - first)
                    return up

                def evict_square(tile, ps, done, first=first):
                    t = tmp.take()
                    a = times_rstd(t.ap, ps, done, t.free)
                    g = dve.do(lambda e: e.scalar_tensor_tensor(t.ap, t.ap, 0.0, t.ap, ALU.max, ALU.mult), a)
                    t.free = split(t.ap, g, hid, tile - first)
                    return a

                def evict_out(j, ps, done, last=first + n == n_hidden):
                    step = add_residual(j, ps, done, scale)
                    if last:
                        after_tile(j)
                    return step

                hid.ready = {}
                gemm(w_in, DT, swiglu_groups(first, n) if gated else pairs(first, n), inp,
                     evict_gated if gated else evict_square)
                gemm(w_out, n, pairs(0, DT), hid, evict_out)

        soft = Ring([Buf(soft_sb[:, i, :]) for i in range(4)])

        def softmax_rest(p, width, src_ap, exp_scale, top, top_scale, c):
            neg = dve.do(lambda e: e.tensor_scalar(c.ap[:, 1:2], c.ap[:, 0:1], top_scale, None, ALU.mult), top)
            pw = p.ap[:, 0:width]
            ex = act.do(lambda e: e.activation(pw, src_ap, ACT.Exp, bias=c.ap[:, 1:2], scale=exp_scale,
                                               accum_out=c.ap[:, 2:3]), [neg, p.free])
            inv = dve.do(lambda e: e.reciprocal(c.ap[:, 3:4], c.ap[:, 2:3]), ex)
            got = dve.do(lambda e: e.tensor_scalar(pw, pw, c.ap[:, 3:4], None, ALU.mult), inv)
            c.free = [got]
            p.ready = [got]
            return ex

        def softmax_biased(p, width, ps_ap, bias_ap, ready):
            c = soft.take()
            pw = p.ap[:, 0:width]
            top = dve.do(lambda e: e.tensor_tensor_reduce(pw, ps_ap, bias_ap, FDH ** -0.5, LOWEST, ALU.add,
                                                          ALU.max, c.ap[:, 0:1]),
                         [ready, p.free, c.free])
            softmax_rest(p, width, pw, 1.0, top, -1.0, c)
            return top

        def turn_p(p, blocks, pt, turn_, at=0):
            for b in range(blocks):
                t = pe.do(lambda e, b=b: e.transpose(turn_.ap[:, b * P:(b + 1) * P],
                                                     p.ap[:, at + b * P:at + (b + 1) * P], ident[:]),
                          [p.ready, turn_.free])
            cp = act.do(lambda e: e.activation(pt.ap[:, at:at + blocks * P], turn_.ap[:, 0:blocks * P], ACT.Copy),
                        [t, pt.free])
            turn_.free = [cp]
            return t, cp

        fq, fk, rq, rk, srg, gate = [tiles(m[n]) for n in ("fq", "fk", "rq", "rk", "srg", "gate")]
        fv, rv, decay, rope, sel = m["fv"], m["rv"], m["decay"], m["rope"], m["sel"]
        p1, pt1 = [Ring([Buf(t) for t in tiles(m[n])]) for n in ("p_1", "pt_1")]
        negc = Buf(m["negc"][:])
        decay_loaded = [load(decay[:], decay_in, sem("decay_loaded"))]
        table_sem = sem("mixing_tables_loaded")

        def mixing1(l):
            fox = Pair(tiles(m["fox_hi"]), tiles(m["fox_lo"]))
            ret = Pair(tiles(m["ret_hi"]), tiles(m["ret_lo"]))
            mrg = Pair(tiles(m["mrg_hi"]), tiles(m["mrg_lo_a"]) + tiles(m["mrg_lo_b"]))
            ready = {}
            tables = [load(rope[:], rope_in, table_sem, [region_free, silu_free()]),
                      load(sel[0:FH, :], sel_in, table_sem, [region_free, silu_free()])]

            def evict_q(dst, key):
                def evict(j, ps, done):
                    ready[key, j] = times_rstd(dst[j], ps, done)
                    return ready[key, j]
                return evict

            def evict_v(dst, key, tok_cols=0):
                def evict(which, ps, done):
                    group, t = which
                    at = group[0] * P
                    step = act.do(lambda e: e.activation(dst[:, t, at:at + 256], ps, ACT.Copy,
                                                         scale=rcol.ap[:, t:t + 1]), [done, rcol.ready])
                    ready[key, t, group[0]] = step
                    rcol.free = [rcol.free, step]
                    return step
                return evict

            def evict_f(j, ps, done):
                f = tmp.take()
                a, b = tmp.take(), ssum
                fa, aa, ba = f.ap[0:FH, :], a.ap[0:FH, :], b.ap[0:FH, :]
                x = dve.do(lambda e: e.tensor_tensor(fa, ps[0:FH, :], rstd.ap[0:FH, :], ALU.mult),
                           [done, rstd.ready, f.free])
                x2 = dve.do(lambda e: e.tensor_scalar(fa, fa, col("b_forget", l, FH), None, ALU.add), x)
                ab = dve.do(lambda e: e.scalar_tensor_tensor(aa, fa, -1.0, fa, ALU.mult, ALU.max), [x2, a.free])
                ex = act.do(lambda e: e.activation(aa, aa, ACT.Exp, scale=-1.0), ab)
                ln = act.do(lambda e: e.activation(aa, aa, ACT.Ln, bias=1.0), ex)
                sp_ = dve.do(lambda e: e.scalar_tensor_tensor(aa, fa, 0.0, aa, ALU.min, ALU.subtract), ln)
                ng = dve.do(lambda e: e.tensor_scalar(aa, aa, -1.0, None, ALU.mult), sp_)
                sc = dve.do(lambda e: e.tensor_tensor_scan(ba, aa, aa, 0.0, ALU.add, ALU.max),
                            [ng, ssum.free])
                f.free, a.free = [sp_], [sc]
                ready["c"] = sc
                return x

            def evict_rope(dst, key, table):
                def evict(j, ps, done):
                    t, u = tmp.take(), tmp.take()
                    x = times_rstd(t.ap, ps, done, t.free)
                    s1 = act.do(lambda e: e.activation(u.ap[0:64, :], t.ap[64:128, :], ACT.Copy), [x, u.free])
                    s2 = act.do(lambda e: e.activation(u.ap[64:128, :], t.ap[0:64, :], ACT.Copy), [x, u.free])
                    c = pool.do(lambda e: e.tensor_tensor(t.ap, t.ap, rope[:, table, :], ALU.mult), [s2, tables])
                    d = pool.do(lambda e: e.tensor_tensor(u.ap, u.ap, rope[:, table + 1, :], ALU.mult), [s2, tables])

                    def add():
                        ready[key, j] = dve.do(lambda e: e.tensor_tensor(dst[j], t.ap, u.ap, ALU.add), [c, d])
                        t.free = u.free = [ready[key, j]]
                    soon.append(add)
                    return x
                return evict

            def evict_rg(j, ps, done):
                t, u = tmp.take(), tmp.take()
                x = times_rstd(t.ap, ps, done, t.free)
                th = act.do(lambda e: e.activation(u.ap, t.ap, ACT.Tanh, scale=0.5), [x, u.free])

                def product():
                    ready["srg", j] = dve.do(lambda e: e.scalar_tensor_tensor(srg[j], u.ap, 1.0, t.ap,
                                                                              ALU.add, ALU.mult), th)
                    t.free = u.free = [ready["srg", j]]
                put_off(product)
                return x

            def evict_gate(j, ps, done):
                t = tmp.take()
                x = times_rstd(t.ap, ps, done, t.free)
                ready["gate", j] = act.do(lambda e: e.activation(gate[j], t.ap, ACT.Tanh, scale=0.5),
                                          [x, tables_used])
                t.free = [ready["gate", j]]
                return x

            tables_used = []

            state = {}

            def fox_scores(n):
                h, i = divmod(n, TT)
                base, j, keys = 64 * (h % 2), h // 2, (i + 1) * P
                if i == 0:
                    b = pe.do(lambda e: e.matmul(turn.ap, sel[0:FH, h * P:(h + 1) * P], ssum.ap[0:FH, :],
                                                 start=True, stop=True), [ready["c"], tables, turn.free])
                    ssum.free = [b]
                    negc.ready = [act.do(lambda e: e.activation(negc.ap, turn.ap, ACT.Copy, scale=FDH ** 0.5),
                                         [b, negc.free])]
                    turn.free = negc.ready
                sc, p = score[n % 2], p1.take()
                qk = pe.do(lambda e: e.matmul(sc.ap[:, 0:keys], fq[j][base:base + 64, i * P:(i + 1) * P],
                                              fk[j][base:base + 64, 0:keys], start=True, stop=False,
                                              skip_group_check=True),
                           [ready["fq", j], ready["fk", j], sc.free])
                mk = pe.do(lambda e: e.matmul(sc.ap[:, i * P:keys], ident[:], tri[:], start=False, stop=True,
                                              skip_group_check=True), first_loads)
                top = softmax_biased(p, keys, sc.ap[:, 0:keys], negc.ap[:, 0:keys], [mk, negc.ready])
                sc.free, negc.free = [top], [top]
                state[n] = p

            def fox_turn(n):
                h, i = divmod(n, TT)
                p, pt = state[n], pt1.take()
                t, cp = turn_p(p, i + 1, pt, turn)
                p.free, pt.ready = [t], [cp]
                state[n] = pt

            def fox_values(n):
                h, i = divmod(n, TT)
                base, j, pt = 64 * (h % 2), h // 2, state.pop(n)
                for b in range(i + 1):
                    g = pe.do(lambda e, b=b: e.matmul(outp.ap[base:base + 64, i * P:(i + 1) * P],
                                                      fv[:, b, h * FDH:(h + 1) * FDH],
                                                      pt.ap[:, b * P:(b + 1) * P], start=b == 0, stop=b == i,
                                                      skip_group_check=True),
                              [pt.ready, ready["fv", b, h // 4 * 2], outp.free])
                pt.free = [g]
                if h % 2 and i == TT - 1:
                    outp.free = split(outp.ap, g, fox, j)

            def ret_scores(n):
                h, i = divmod(n, TT)
                w_, p, sc = S - i * P, p1.take(), score[n % 2]
                qk = pe.do(lambda e: e.matmul(sc.ap[:, 0:w_], rk[h][:, i * P:(i + 1) * P], rq[h][:, i * P:S],
                                              start=True, stop=True, skip_group_check=True),
                           [ready["rq", h], ready["rk", h], sc.free])
                p.ready = [dve.do(lambda e: e.tensor_tensor(p.ap[:, 0:w_], sc.ap[:, 0:w_], decay[:, h, 0:w_],
                                                            ALU.mult), [qk, p.free, decay_loaded])]
                sc.free = p.ready
                state["r", n] = p

            def ret_values(n):
                h, i = divmod(n, TT)
                w_, p = S - i * P, state.pop(("r", n))
                g = pe.do(lambda e: e.matmul(outp.ap[:, i * P:S], rv[:, i, h * P:(h + 1) * P], p.ap[:, 0:w_],
                                             start=i == 0, stop=i == TT - 1, skip_group_check=True),
                          [p.ready, ready["rv", i, h // 2 * 2], outp.free])
                p.free = [g]
                if i == TT - 1:
                    o, sq = pt1.take(), pt1.take()
                    c1 = act.do(lambda e: e.activation(sq.ap, outp.ap, ACT.Square), [g, sq.free])
                    c2 = act.do(lambda e: e.activation(o.ap, outp.ap, ACT.Copy), [g, o.free])
                    outp.free = [c2]
                    sq.ready, sq.free, o.ready, o.free = [c1], [], [c2], []
                    state["o", h] = o, sq

            def ret_stats(h):
                stats(state["o", h][1], hcol, tok_tiles, P)

            def ret_finish(h):
                o, _ = state.pop(("o", h))
                b = Buf(tmp.take().ap)
                tb = tmp.bufs[(tmp.n - 1) % NTMP]
                b.free = tb.free
                spread(hcol, b, half=True)
                g = pool.do(lambda e: e.tensor_tensor(o.ap, o.ap, srg[h], ALU.mult), [o.ready, ready["srg", h]])
                y = dve.do(lambda e: e.scalar_tensor_tensor(b.ap, o.ap, col("ret_norm", RH * l + h), b.ap,
                                                            ALU.mult, ALU.mult), [g, b.ready])
                o.free = [y]
                tb.free = split(b.ap, y, ret, h)

            def later(fn, *args):
                return lambda: fn(*args)

            def chain(n_steps, *stages_):
                for n in range(n_steps + len(stages_) - 1):
                    def slot(n=n):
                        for k, stage in enumerate(stages_):
                            if 0 <= n - k < n_steps:
                                stage(n - k)
                    filler.append(slot)

            name = f"mix{l}"
            norm_hooks(ssum, rcol, rstd)
            rate[0] = 0
            gemm(name, DT, pairs(0, 4), inp, evict_q(fq, "fq"))
            gemm(name, DT, [[0]], inp, evict_f)
            gemm(name, DT, pairs(0, 4), inp, evict_q(fk, "fk"))
            gemm(name, DT, pairs(0, 4), inp, evict_v(fv, "fv"), rows=tok_tiles)
            flush()
            for n in range(FH * TT + 2):
                def fox_slot(n=n):
                    if n < FH * TT:
                        fox_scores(n)
                    if n >= 2:
                        fox_values(n - 2)
                    if 0 <= n - 1 < FH * TT:
                        fox_turn(n - 1)
                filler.append(fox_slot)


            def ret_end(n):
                if n % TT == TT - 1:
                    ret_stats(n // TT)

            def ret_end2(n):
                if n % TT == TT - 1:
                    ret_finish(n // TT)
            chain(RH * TT, ret_scores, ret_values, ret_end, ret_end2)
            rate[0] = 2
            gemm(name, DT, pairs(0, RH), inp, evict_rope(rq, "rq", 0))
            gemm(name, DT, pairs(0, RH), inp, evict_rope(rk, "rk", 2))
            gemm(name, DT, pairs(0, 4), inp, evict_v(rv, "rv"), rows=tok_tiles)
            gemm(name, DT, pairs(0, RH), inp, evict_rg)
            tables_used += [ready["rk", RH - 1]]
            gemm(name, DT, pairs(0, 2 * DT), inp, evict_gate)
            flush()
            drain()
            rate[0] = 1

            def evict_ret(j, ps, done):
                ready["m", j] = dve.do(lambda e: e.scalar_tensor_tensor(gate[j], gate[j], 1.0, ps, ALU.add, ALU.mult),
                                       [done, ready["gate", j]])
                return ready["m", j]

            def evict_fox(j, ps, done):
                g = gate[DT + j]
                u = dve.do(lambda e: e.scalar_tensor_tensor(g, g, 1.0, ps, ALU.add, ALU.mult),
                           [done, ready["gate", DT + j]])
                s_ = pool.do(lambda e: e.tensor_tensor(gate[j], gate[j], g, ALU.add), [u, ready["m", j]])
                split(gate[j], s_, mrg, j)
                return u

            for j in range(0, DT, 2):
                gemm(f"w_o_ret{l}", RH, [[j, j + 1]], ret, evict_ret)
                gemm(f"w_o_fox{l}", 4, [[j, j + 1]], fox, evict_fox)

            def evict_out(j, ps, done):
                step = add_residual(j, ps, done, 0.5)
                norm_tile(j, "norm_ffn2", ssum, DT * l)
                return step
            gemm(f"w_out{l}", DT, pairs(0, DT), mrg, evict_out)
            region_free[:] = [mrg.used]

        region_free = []

        def silu_free():
            return [b.free for b in silu.bufs]

        scratch = nc.dram_tensor("bias_by_distance", [3 * GH, 2 * S], F32, kind="Internal").ap()
        onehot, rel = m["onehot"], m["rel"]
        bias_loads = [load(onehot[0:NB], onehot_in, bias_sem), load(rel[0:GH], band_in, bias_sem),
                      load(table_sb[0:NB, :], table_in, bias_sem)]
        bias_stores = []
        for g in range(3):
            for half in range(2):
                b = (bank + score)[2 * g + half]
                cut = slice(half * S, half * S + S)
                t = pe.do(lambda e, g=g, b=b, cut=cut: e.matmul(b.ap[0:GH, :], table_sb[0:NB, g * GH:(g + 1) * GH],
                                                                onehot[0:NB, g, cut], start=True, stop=True),
                          bias_loads)
                r_ = dve.do(lambda e, g=g, b=b, cut=cut: e.scalar_tensor_tensor(
                    rel[0:GH, g, cut], b.ap[0:GH, :], GD ** 0.5, rel[0:GH, g, cut], ALU.mult, ALU.add), [t, bias_loads])
                b.free = [r_]
            bias_stores.append(load(scratch[g * GH:(g + 1) * GH, :], rel[0:GH, g, :], bias_sem, [r_]))
        WIDE, NEAR = 2 * S, 2 * P
        wide = nc.dram_tensor("bias_rows_wide", [GH, P * (WIDE + DIL)], F32, kind="Internal").ap()
        near = nc.dram_tensor("bias_rows_near", [2 * GH, P * (NEAR + 1)], F32, kind="Internal").ap()
        bias_rows = []

        def lay_bias_rows():
            for gh in range(3 * GH):
                if gh < GH:
                    dst = wide[gh, :].rearrange("(j y) -> j y", j=P)[:, 0:WIDE]
                    src = bass.AP(tensor=scratch.tensor, offset=gh * 2 * S, ap=[[0, P], [1, WIDE]])
                else:
                    dst = near[gh - GH, :].rearrange("(j y) -> j y", j=P)[:, 0:NEAR]
                    src = bass.AP(tensor=scratch.tensor, offset=gh * 2 * S + S - P, ap=[[0, P], [1, NEAR]])
                bias_rows.append(load(dst, src, bias_sem, bias_stores))

        region_free[:] = bias_stores
        for b in silu.bufs:
            b.free = [t]

        lam = vec[:, VEC["lru_lambda_2"][0]:VEC["lru_lambda_2"][0] + RT]
        lv = [lruv[:, i, :] for i in range(10)]

        def small_op(fn, after):
            return dve.do(fn, [after, first_loads])
        st = small_op(lambda e: e.scalar_tensor_tensor(lv[0], lam, -1.0, lam, ALU.mult, ALU.max), [])
        st = act.do(lambda e: e.activation(lv[1], lv[0], ACT.Exp, scale=-1.0), st)
        st = small_op(lambda e: e.tensor_scalar(lv[2], lv[1], 2.0, None, ALU.add), st)
        st = small_op(lambda e: e.reciprocal(lv[3], lv[2]), st)
        st = small_op(lambda e: e.tensor_tensor(lv[4], lv[1], lv[3], ALU.mult), st)
        st = small_op(lambda e: e.tensor_tensor(lv[5], lv[4], lv[4], ALU.mult), st)
        st = small_op(lambda e: e.tensor_scalar(lv[6], lv[5], 1.0 / 15, None, ALU.mult), st)
        for k in (13, 11, 9, 7, 5, 3):
            st = small_op(lambda e, k=k: e.scalar_tensor_tensor(lv[6], lv[6], 1.0 / k, lv[5], ALU.add, ALU.mult), st)
        st = small_op(lambda e: e.scalar_tensor_tensor(lv[6], lv[6], 1.0, lv[4], ALU.add, ALU.mult), st)
        st = small_op(lambda e: e.tensor_scalar(lv[7], lam, -1.0, 0.0, ALU.mult, ALU.max), st)
        st = small_op(lambda e: e.scalar_tensor_tensor(lv[8], lv[6], 2.0, lv[7], ALU.mult, ALU.add), st)
        st = small_op(lambda e: e.tensor_scalar(lv[9], lv[8], -8.0, None, ALU.mult), st)
        c8_ready = small_op(lambda e: e.tensor_scalar(lv[8], lv[8], 8.0, None, ALU.mult), st)
        bg = VEC["b_gate_2"][0]
        half_ready = small_op(lambda e: e.tensor_scalar(halfb[:], vec[:, bg:bg + 3 * DT], 0.5, None, ALU.mult), [])

        memp = Pair(tiles(m["mem_hi"]), tiles(m["mem_lo"]))
        memx, mem_rstd, mem_ssum = tiles(m["memx"]), Buf(m["mem_rstd"][:]), Buf(m["mem_ssum"][:])
        mem_rows = tok_tiles[:NMEM // P]
        mk, mv = tiles(m["mk"]), m["mv"]
        got = {}

        def prepare_memory(after):
            x = load(m["memx"][:], mem_in, sem("memory_loaded"), after)
            for j in range(DT):
                split(memx[j], x, memp, j, scale=col("g_mem_2", j))
                square_sum(memx[j], x, j, mem_ssum)
            norm_hooks(mem_ssum, mcol, mem_rstd, mem_rows)

        def memory_keys():
            def evict(j, ps, done):
                got["mk", j] = dve.do(lambda e: e.tensor_tensor(mk[j], ps, mem_rstd.ap, ALU.mult),
                                      [done, mem_rstd.ready])
                return got["mk", j]
            gemm("mem", DT, pairs(0, MH), memp, evict, n=NMEM)

        def memory_values():
            def evict(which, ps, done):
                group, t = which
                at = group[0] * P
                step = act.do(lambda e: e.activation(mv[:, t, at:at + 256], ps, ACT.Copy, scale=mcol.ap[:, t:t + 1]),
                              [done, mcol.ready])
                got["mv", t, group[0]] = step
                return step
            gemm("mem", DT, pairs(0, MH), memp, evict, rows=mem_rows)

        def apply_norm(j, gain):
            x = xT[j]
            step = dve.do(lambda e: e.scalar_tensor_tensor(x.ap, x.ap, col(gain, j), rstd.ap, ALU.mult, ALU.mult),
                          [x.ready, x.free, rstd.ready])
            rstd.free, x.ready, x.free = [step], [step], []

        def mixing2():
            dq, dk, mq, dv = tiles(m["dq"]), tiles(m["dk"]), tiles(m["mq"]), m["dv"]
            p2 = Ring([Buf(t) for t in tiles(m["p_2"])])
            pt2 = Buf(m["pt_2"][:])
            bias = Ring([Buf(t) for t in tiles(m["bias"])])
            pad, rgw = Buf(m["pad"][:]), Ring([Buf(t) for t in tiles(m["rgw"])])
            lru_x, lru_g = tiles(m["lru_x"]), tiles(m["lru_g"])
            lru = Pair(tiles(m["lru_hi"]), tiles(m["lru_lo"]))
            dil = Pair(tiles(m["dil_hi"]), tiles(m["dil_lo"]))
            memo = Pair(tiles(m["memo_hi"]), tiles(m["memo_lo"]))
            mrg = Pair(tiles(m["mrg2_hi"]), tiles(m["mrg2_lo"]))
            acc, gate2 = tiles(m["acc"]), tiles(m["gate2"])
            ready, state = got, {}

            def evict_q(dst, key):
                def evict(j, ps, done):
                    ready[key, j] = times_rstd(dst[j], ps, done)
                    return ready[key, j]
                return evict

            def evict_dv(g):
                def evict(which, ps, done):
                    t = which[1]
                    c = t if g == 0 else TT + t
                    step = act.do(lambda e: e.activation(dv[:, t, g, :], ps, ACT.Copy, scale=rcol.ap[:, c:c + 1]),
                                  [done, rcol.ready])
                    ready["dv", t, g] = step
                    rcol.free = [rcol.free, step]
                    return step
                return evict

            def head_at(g, h):
                return (g * GH + h) // 2, GD * (h % 2)

            def load_bias(n):
                h, r = divmod(n, DIL)
                b = bias.take()
                b.ready = []
                parts = [(0, wide[h, 0:P * WIDE].rearrange("(j y) -> j y", j=P)[:, S - 1 - r:2 * S - 1 - r])]
                parts += [(S + i * P, near[i * GH + h, 0:P * NEAR].rearrange("(j y) -> j y", j=P)[:, P - 1:2 * P - 1])
                          for i in range(2)]
                for at, src in parts:
                    b.ready.append(load(b.ap[:, at:at + src.shape[1]], src, tile_sem[n % 2], [b.free, bias_rows]))
                state["bias", n] = b

            def dil_scores(n):
                h, r = divmod(n, DIL)
                if n == 0:
                    load_bias(0)
                if n + 1 < GH * DIL:
                    load_bias(n + 1)
                b, p = state.pop(("bias", n)), p2.take()
                for g, (at, width) in enumerate(((0, S), (S, P), (S + P, P))):
                    j, base = head_at(g, h)
                    q = dq[j][base:base + GD, r::DIL]
                    k = dk[j][base:base + GD, :] if g == 0 else dk[j][base:base + GD, r::DIL]
                    qk = pe.do(lambda e, q=q, k=k, at=at, width=width: e.matmul(
                        score_ps[:, at:at + width], q, k, start=True, stop=True, skip_group_check=True),
                        [ready["dq", j], ready["dk", j], score[0].free, score[1].free])
                top = softmax_biased(p, 768, score_ps[:, 0:768], b.ap, [qk, b.ready])
                score[0].free = score[1].free = b.free = [top]
                state[n] = p

            def dil_values(n):
                h, r = divmod(n, DIL)
                base = GD * (h % 2)
                vs = [dv[:, t, 0, h * GD:(h + 1) * GD] for t in range(TT)]
                vs += [dv[:, r, g, h * GD:(h + 1) * GD] for g in (1, 2)]
                for b, v in enumerate(vs):
                    g_ = pe.do(lambda e, b=b, v=v: e.matmul(outp.ap[base:base + GD, r * P:(r + 1) * P], v,
                                                            pt2.ap[:, b * P:(b + 1) * P], start=b == 0,
                                                            stop=b == 5, skip_group_check=True),
                               [pt2.ready, outp.free, [ready["dv", t, 0] for t in range(TT)],
                                ready["dv", r, 1], ready["dv", r, 2]])
                pt2.free = [g_]
                if h % 2 and r == DIL - 1:
                    j = h // 2
                    src = outp.ap.rearrange("p (r j) -> p r j", r=DIL)
                    hi_v = dil.hi[j].rearrange("p (j r) -> p r j", r=DIL)
                    lo_v = dil.lo[j].rearrange("p (j r) -> p r j", r=DIL)
                    hi = act.do(lambda e: e.activation(hi_v, src, ACT.Copy), g_)
                    lo = dve.do(lambda e: e.tensor_tensor(lo_v, src, hi_v.bitcast(F32), ALU.subtract), [g_, hi])
                    dil.ready[j] = outp.free = [hi, lo]

            def turn_first(n, blocks):
                p = state[n]
                t, cp = turn_p(p, blocks, pt2, turn)
                p.free, pt2.ready = [t], [cp]

            def turn_rest(n):
                p = state.pop(n)
                t, cp = turn_p(p, 2, pt2, turn, at=4 * P)
                p.free, pt2.ready = [t], [cp]

            def mem_scores(n):
                h, i = divmod(n, TT)
                sc, p, c = score[n % 2], p2.take(), soft.take()
                ps = sc.ap[:, 0:NMEM]
                qk = pe.do(lambda e: e.matmul(ps, mq[h][:, i * P:(i + 1) * P], mk[h], start=True, stop=True,
                                              skip_group_check=True), [ready["mq", h], ready["mk", h], sc.free])
                top = dve.do(lambda e: e.tensor_reduce(c.ap[:, 0:1], ps, AX.X, ALU.max), [qk, c.free])
                ex = softmax_rest(p, NMEM, ps, P ** -0.5, top, -(P ** -0.5), c)
                sc.free = [top, ex]
                state[n] = p

            def mem_values(n):
                h, i = divmod(n, TT)
                for b in range(2):
                    g_ = pe.do(lambda e, b=b: e.matmul(outp.ap[:, i * P:(i + 1) * P], mv[:, b, h * P:(h + 1) * P],
                                                       pt2.ap[:, b * P:(b + 1) * P], start=b == 0, stop=b == 1,
                                                       skip_group_check=True),
                               [pt2.ready, outp.free, ready["mv", b, h // 2 * 2]])
                pt2.free = [g_]
                if i == TT - 1:
                    ready["mo", h] = act.do(lambda e: e.activation(mq[h], outp.ap, ACT.Copy), g_)
                    outp.free = [ready["mo", h]]
                state["last"] = g_

            def slots(n_steps, scores, first, rest, values):
                for n in range(n_steps + 2):
                    def slot(n=n):
                        if n < n_steps:
                            scores(n)
                        if 0 <= n - 2:
                            values(n - 2)
                        if 0 <= n - 1 < n_steps:
                            first(n - 1)
                            if rest:
                                rest(n - 1)
                    filler.append(slot)

            pad_zero = dve.do(lambda e: e.memset(pad.ap[:, 0:3], 0.0), region_free)

            def evict_lru(tile, ps, done):
                if tile < RT:
                    j = tile
                    x = times_rstd(pad.ap[:, 3:3 + S], ps, done, [pad.free, pad_zero])
                    y = lru_x[j]
                    s_ = dve.do(lambda e: e.tensor_scalar(y, pad.ap[:, 0:S], col("conv_w_2", j), col("conv_b_2", j),
                                                          ALU.mult, ALU.add), x)
                    for k in range(1, 4):
                        s_ = dve.do(lambda e, k=k: e.scalar_tensor_tensor(
                            y, pad.ap[:, k:k + S], col("conv_w_2", RT * k + j), y, ALU.mult, ALU.add), s_)
                    pad.free = [s_]
                    ready["x", j] = s_
                    return x
                j = tile - 100
                t = tmp.take()
                a = times_rstd(t.ap, ps, done, t.free)
                ready["g", j] = act.do(lambda e: e.activation(lru_g[j], t.ap, ACT.Gelu_apprx_tanh), a)
                t.free = [ready["g", j]]
                if j:
                    hooks.append(lambda: (recur_scan(j - 1), recur_gates(j)))
                else:
                    hooks.append(lambda: recur_gates(j))
                hooks.append(lambda: recur_factor(j))
                if j == RT - 1:
                    hooks.append(lambda: recur_scan(j))
                return a

            def recur_gates(j):
                wb, x = rgw.take(), lru_x[j]
                wl = load(wb.ap, rg_in[j], rg_sem[j % 2], wb.free)
                ps = []
                for k in range(2):
                    sc = score[k]
                    ps.append(pe.do(lambda e, sc=sc, k=k: e.matmul(sc.ap, wb.ap[:, k * P:(k + 1) * P], x,
                                                                   start=True, stop=True),
                                    [wl, ready["x", j], sc.free]))
                wb.free = [ps[1]]
                r_, i_, u, a2 = [tmp.take() for _ in range(4)]
                c8, nc8 = lv[8][:, j:j + 1], lv[9][:, j:j + 1]
                s1 = act.do(lambda e: e.activation(r_.ap, score[0].ap, ACT.Sigmoid, bias=col("b_rg_a_2", j)),
                            [ps[0], r_.free])
                s2 = act.do(lambda e: e.activation(i_.ap, score[1].ap, ACT.Sigmoid, bias=col("b_rg_x_2", j)),
                            [ps[1], i_.free])
                score[0].free, score[1].free = [s1], [s2]
                s3 = act.do(lambda e: e.activation(u.ap, r_.ap, ACT.Tanh, scale=c8), [s1, c8_ready, u.free])
                ix = pool.do(lambda e: e.tensor_tensor(i_.ap, i_.ap, x, ALU.mult), [s2])
                s4 = act.do(lambda e: e.activation(r_.ap, r_.ap, ACT.Exp, scale=nc8), [s1, s3, c8_ready])
                s5 = act.do(lambda e: e.activation(a2.ap, r_.ap, ACT.Square), [s4, a2.free])
                state["lru", j] = (r_, i_, u, a2, s3, s4, s5, ix, ps[1])

            def recur_factor(j):
                r_, i_, u, a2, s3, s4, s5, ix, last_ps = state.pop(("lru", j))
                v = dve.do(lambda e: e.scalar_tensor_tensor(u.ap, a2.ap, 1.0, u.ap, ALU.add, ALU.mult), [s5, s3])
                mu = act.do(lambda e: e.activation(u.ap, u.ap, ACT.Sqrt), v)
                b = pool.do(lambda e: e.tensor_tensor(i_.ap, i_.ap, u.ap, ALU.mult), [mu, ix])
                u.free = [b]
                state["lru2", j] = (r_, i_, a2, s4, v, b, ix, last_ps)

            def recur_scan(j):
                r_, i_, a2, s4, v, b, ix, last_ps = state.pop(("lru2", j))
                h = dve.do(lambda e: e.tensor_tensor_scan(a2.ap, r_.ap, i_.ap, 0.0, ALU.mult, ALU.add), [b, s4, v])
                y = dve.do(lambda e: e.tensor_tensor(a2.ap, a2.ap, lru_g[j], ALU.mult), [h, ready["g", j]])
                r_.free = i_.free = [h]
                lru.used = [y, last_ps, ix]
                a2.free = split(a2.ap, y, lru, j)

            norm_hooks(ssum, rcol, rstd, tok_tiles + res_tiles)
            rate[0] = 0
            gemm("mixb", DT, pairs(0, MH), inp, evict_q(mq, "mq"))
            gemm("mixb", DT, pairs(0, 6), inp, evict_q(dq, "dq"))
            gemm("mixb", DT, pairs(0, 6), inp, evict_q(dk, "dk"))
            for g in range(3):
                gemm("mixb", DT, [[0, 1]], inp, evict_dv(g), rows=tok_tiles if g == 0 else res_tiles)
            flush()
            slots(GH * DIL, dil_scores, lambda n: turn_first(n, 4), turn_rest, dil_values)
            slots(MH * TT, mem_scores, lambda n: turn_first(n, 2), None, mem_values)
            rate[0] = 3
            gemm("mixb", DT, [[j, 100 + j] for j in range(RT)], inp, evict_lru)
            flush()
            while hooks:
                hooks.popleft()()
            drain()
            rate[0] = 1
            memo.used = [state["last"]]
            for h in range(MH):
                split(mq[h], ready["mo", h], memo, h)

            def evict_gate(branch, dst):
                def evict(j, ps, done):
                    t = tmp.take()
                    a = times_rstd(t.ap, ps, done, t.free)
                    hb = halfb[:, branch * DT + j:branch * DT + j + 1]
                    ready["th", j] = act.do(lambda e: e.activation(dst[j], t.ap, ACT.Tanh, bias=hb, scale=0.5),
                                            [a, half_ready, ready.get(("merged", j))])
                    t.free = [ready["th", j]]
                    return a
                return evict

            def evict_branch(branch, dst):
                def evict(j, ps, done):
                    y = dve.do(lambda e: e.scalar_tensor_tensor(dst[j], dst[j], 1.0, ps, ALU.add, ALU.mult),
                               [done, ready["th", j]])
                    if branch:
                        y2 = pool.do(lambda e: e.tensor_tensor(acc[j], acc[j], dst[j], ALU.add),
                                     [y, ready["acc", j]])
                        ready["merged", j] = ready["acc", j] = y2
                        if branch == 2:
                            split(acc[j], y2, mrg, j)
                    else:
                        ready["acc", j] = y
                    return y
                return evict

            for branch, (name, n_k, src, dst) in enumerate((("lru_out", RT, lru, acc), ("dil_out", 2, dil, gate2),
                                                            ("mem_out", MH, memo, gate2))):
                for j in range(0, DT, 2):
                    gemm("mixb", DT, [[j, j + 1]], inp, evict_gate(branch, dst))
                    gemm(name, n_k, [[j, j + 1]], src, evict_branch(branch, dst))

            def evict_out(j, ps, done):
                step = add_residual(j, ps, done, 0.5)
                norm_tile(j, "g_mlp_2", ssum)
                return step
            gemm("out_b", DT, pairs(0, DT), mrg, evict_out)

        def squares_only(j):
            xT[j].free = [square_sum(xT[j].ap, xT[j].ready, j, ssum)]

        def program():
            for j in range(DT):
                norm_tile(j, "norm_ffn1", ssum)
            for l in range(DEPTH):
                norm_hooks(ssum, rcol, rstd)
                feed_forward(f"ffn1_in{l}", f"ffn1_out{l}", FF // P, True, 0.5,
                             lambda j, l=l: norm_tile(j, "norm_mix", ssum, DT * l))
                if l == 0:
                    lay_bias_rows()
                mixing1(l)
                norm_hooks(ssum, rcol, rstd)
                if l + 1 == DEPTH:
                    prepare_memory(region_free)
                feed_forward(f"ffn2_in{l}", f"ffn2_out{l}", FF // P, True, 0.5,
                             (lambda j, l=l: norm_tile(j, "norm_ffn1", ssum, DT * (l + 1))) if l + 1 < DEPTH
                             else squares_only)
            hooks.extend([lambda: None, lambda: stats(ssum, rcol, tok_tiles), lambda: spread(rcol, rstd)])
            memory_keys()
            for j in range(DT):
                apply_norm(j, "norm_final")
                norm_tile(j, "g_mix_2", ssum)
            memory_values()
            mixing2()
            norm_hooks(ssum, rcol, rstd)
            feed_forward("mlp_in", "mlp_out", FF2 // P, False, 1.0, squares_only)
            flush()
            stats(ssum, rcol, tok_tiles)
            spread(rcol, rstd)
            for j in range(DT):
                apply_norm(j, "g_final_2")

        Units.places += [(act.place(), dve.place()) for _ in range(AHEAD)]
        Units.load_places += [sp.place() for _ in range(AHEAD + 2)]
        program()
        flush()
        stores = [load(out[:, j, :], xT[j].ap, out_sem, [xT[j].ready]) for j in range(DT)]

        count(lanes)
        stored = stores[-1].value
        block = ctx.enter_context(nc.Block())

        @block.sync
        def _(eng):
            emit(sp, eng)
            eng.wait_ge(out_sem, stored)

        @block.gpsimd
        def _(eng):
            emit(pool, eng)

        @block.scalar
        def _(eng):
            emit(act, eng)

        @block.vector
        def _(eng):
            emit(dve, eng)

        @block.tensor
        def _(eng):
            emit(pe, eng)


RET, FOX = RH * P, FH * FDH
MIX_AT = dict(rq=0, rk=RET, rv=2 * RET, rg=3 * RET, fq=4 * RET, fk=4 * RET + FOX, fv=4 * RET + 2 * FOX,
              ff=4 * RET + 3 * FOX, gates=4 * RET + 3 * FOX + FH)


QKV = 3 * GH * GD
MIX2_AT = dict(x=0, g=RNN, dq=2 * RNN, dk=2 * RNN + QKV, dv=2 * RNN + 2 * QKV, mq=2 * RNN + 3 * QKV,
               gates=2 * RNN + 3 * QKV + MH * P)


def starts(first_col, groups):
    return [[first_col + t * P for t in g] for g in groups]


def plans():
    out = {}
    for l in range(DEPTH):
        for k in (1, 2):
            pieces = ffn_pieces(FF // P)
            out[f"ffn{k}_in{l}"] = (f"w_ffn{k}_in", l, [(0, DT, starts(0, swiglu_groups(a, n))) for a, n in pieces])
            out[f"ffn{k}_out{l}"] = (f"w_ffn{k}_out", l, [(a, n, starts(0, pairs(0, DT))) for a, n in pieces])
        c = MIX_AT
        four = pairs(0, 4)
        out[f"mix{l}"] = ("w_in", l, [(0, DT, starts(c["fq"], four) + [[c["ff"]]] + starts(c["fk"], four)
                                       + starts(c["fv"], four) + starts(c["rq"], four) + starts(c["rk"], four)
                                       + starts(c["rv"], four) + starts(c["rg"], four)
                                       + starts(c["gates"], pairs(0, 2 * DT)))])
        out[f"w_o_ret{l}"] = ("w_o_ret", l, [(0, RH, starts(0, pairs(0, DT)))])
        out[f"w_o_fox{l}"] = ("w_o_fox", l, [(0, 4, starts(0, pairs(0, DT)))])
        out[f"w_out{l}"] = ("w_out", l, [(0, DT, starts(0, pairs(0, DT)))])
    c = MIX2_AT
    mem = pairs(0, MH)
    out["mem"] = ("w_mem_kv_2", None, [(0, DT, starts(0, mem) + starts(MH * P, mem))])
    mix = starts(c["mq"], mem) + starts(c["dq"], pairs(0, 6)) + starts(c["dk"], pairs(0, 6))
    mix += starts(c["dv"], pairs(0, 6)) + [[c["x"] + j * P, c["g"] + j * P] for j in range(RT)]
    mix += starts(c["gates"], pairs(0, 3 * DT))
    out["mixb"] = ("w_in_2", None, [(0, DT, mix)])
    for name, src, n_k in (("lru_out", "w_lru_out_2", RT), ("dil_out", "w_dil_out_2", 2),
                           ("mem_out", "w_mem_out_2", MH), ("out_b", "w_out_2", DT)):
        out[name] = (src, None, [(0, n_k, starts(0, pairs(0, DT)))])
    out["mlp_in"] = ("w_mlp_in_2", None, [(0, DT, starts(0, pairs(a, n))) for a, n in ffn_pieces(FF2 // P)])
    out["mlp_out"] = ("w_mlp_out_2", None, [(a, n, starts(0, pairs(0, DT))) for a, n in ffn_pieces(FF2 // P)])
    return out


def pack(w, plan, ff_at=None):
    parts = []
    for k0, nk, groups in plan:
        for g in groups:
            for k, n in unit_blocks(nk, len(g)):
                rows = w[(k0 + k) * P:(k0 + k + n) * P].reshape(n, P, -1)
                cols = []
                for c in g:
                    if c == ff_at:
                        cols.append(np.concatenate([rows[:, :, c:c + FH], np.zeros((n, P, P - FH), w.dtype)], 2))
                    else:
                        cols.append(rows[:, :, c:c + P])
                parts.append(np.concatenate(cols, 2).transpose(1, 0, 2).reshape(-1))
    return np.concatenate(parts)


def constants():
    f = np.float32
    q, k = np.arange(P)[:, None], np.arange(P)[None, :]
    tri = np.where(k <= q, 0.0, NEG).astype(f)
    s_, t = np.arange(P)[:, None], np.arange(S)[None, :]
    gamma = 1.0 - 2.0 ** (-5.0 - np.arange(RH))
    decay = np.stack([np.where(t >= s_, g ** np.maximum(t - s_, 0).astype(np.float64), 0.0) for g in gamma], 1)
    half = P // 2
    inv = np.power(f(10000.0), -np.arange(0, P, 2, dtype=f) / f(P)).astype(f)
    ang = (np.arange(S, dtype=f)[None, :] * inv[:, None]).astype(f)
    cos, sin = np.cos(ang), np.sin(ang)
    cos2, sin2 = np.concatenate([cos, cos]), np.concatenate([-sin, sin])
    rope = np.stack([cos2, sin2, cos2 * f(P ** -0.5), sin2 * f(P ** -0.5)], 1)
    sel = np.zeros((FH, FH, P), f)
    sel[np.arange(FH), np.arange(FH)] = 1.0
    y = np.arange(2 * S) - (S - 1)
    onehot, band = np.zeros((NB, 3, 2 * S), f), np.full((3, 2 * S), NEG, f)
    for g, dist in enumerate((-y, -4 * y, np.where(y % 4 == 0, -4 * y, -1))):
        ok = (dist >= 0) & (dist <= (P, 4 * P, 16 * P)[g]) & (y > -P - (g == 0))
        near = np.maximum(dist, 1).astype(f)
        large = NB // 2 + (np.log(near / f(NB // 2)) / f(np.log(2048 / (NB // 2))) * f(NB // 2)).astype(np.int32)
        bucket = np.where(dist < NB // 2, dist, np.minimum(large, NB - 1))
        onehot[bucket[ok], g, np.nonzero(ok)[0]] = 1.0
        band[g, ok] = 0.0
    band = np.broadcast_to(band, (GH, 3, 2 * S)).copy()
    return dict(onehot_in=onehot, band_in=band, ident_in=np.eye(P, dtype=f), tri_in=tri, decay_in=decay.astype(f), rope_in=rope.astype(f),
                sel_in=sel.reshape(FH, FH * P))


def columns(a):
    return a.reshape(-1, P).T


def small_vectors(x):
    parts = []
    for name, (_, n) in VEC.items():
        a = np.asarray(x[name])
        if name == "b_forget":
            c = np.zeros((P, n), a.dtype)
            c[:FH] = a.T
        else:
            c = columns(a.reshape(-1))
        parts.append(c)
    return np.ascontiguousarray(np.concatenate(parts, 1))


def arrays_of(inputs):
    f = {k: np.asarray(v) for k, v in inputs.items()}
    arrays = dict(constants())
    arrays["x_in"] = np.ascontiguousarray(f["x"][0].T.reshape(DT, P, S).transpose(1, 0, 2))
    arrays["vec_in"] = small_vectors(f)
    arrays["mem_in"] = np.ascontiguousarray(f["mem_2"][0].T.reshape(DT, P, NMEM).transpose(1, 0, 2))
    arrays["table_in"] = np.ascontiguousarray(f["rel_bias_2"])
    rg = np.zeros((RT, P, 2, P), np.float32)
    for k, name in enumerate(("w_rg_a_2", "w_rg_x_2")):
        for b in range(2):
            rg[:, b * 64:b * 64 + 64, k, b * 64:b * 64 + 64] = f[name][b::2]
    arrays["rg_in"] = rg.reshape(RT, P, 2 * P)
    for name, (src, l, plan) in plans().items():
        w = f[src] if l is None else f[src][l]
        arrays["w_" + name] = pack(w, plan, MIX_AT["ff"] if src == "w_in" else None)
    return arrays


ORDER = ["x_in", "vec_in", "ident_in", "tri_in", "decay_in", "rope_in", "sel_in", "mem_in", "onehot_in", "band_in",
         "table_in", "rg_in"]


def kernel(**inputs):
    import concourse.bacc as bacc
    from concourse.bass_utils import run_bass_kernel_spmd

    nc = bacc.Bacc("TRN2", target_bir_lowering=False, num_devices=1)
    arrays = arrays_of(inputs)
    aps = {name: nc.dram_tensor(name, a.shape, mybir.dt.from_np(a.dtype), kind="ExternalInput").ap()
           for name, a in arrays.items()}
    out = nc.dram_tensor("out", (P, DT, S), F32, kind="ExternalOutput").ap()
    w = {name[2:]: ap for name, ap in aps.items() if name.startswith("w_")}
    build(nc, *[aps[name] for name in ORDER], w, out)
    r = run_bass_kernel_spmd(nc, [arrays], core_ids=[0])
    y = r.results[0]["out"]
    return y.transpose(1, 0, 2).reshape(D, S).T.reshape(1, S, D)
```

```python
from collections import deque
from contextlib import ExitStack

import numpy as np
import concourse.bass as bass
from concourse import mybir

P = 128
S = 512
TT = S // P
D = 1024
DT = D // P
EPS = 1e-6
NEG = -1e30
LOWEST = -3.0e38
DEPTH = 2
FF = 2816
RH = 4
FH, FDH = 8, 64
PARTS = 32 + FH
NMEM = 256
MH = 4
RNN = 768
RT = RNN // P
GH, GD = 4, 64
NB = 32
FF2 = 4096
BRANCHES = (2, 0, 1)
DIL = 4

UNIT = 1024
RAW, SPLIT, AHEAD = 3, 3, 2

F32, F32R, I32 = mybir.dt.float32, mybir.dt.float32r, mybir.dt.int32
ALU, ACT = mybir.AluOpType, mybir.ActivationFunctionType
AX = mybir.AxisListType

VEC = {}


def _vec_layout():
    at = 0
    for name, n in (("norm_ffn1", 2 * DT), ("norm_mix", 2 * DT), ("norm_ffn2", 2 * DT), ("norm_final", DT),
                    ("ret_norm", 2 * RH), ("b_forget", 2), ("g_mix_2", DT), ("b_gate_2", 3 * DT),
                    ("conv_w_2", 4 * RT), ("conv_b_2", RT), ("b_rg_a_2", RT), ("b_rg_x_2", RT),
                    ("lru_lambda_2", RT), ("g_mem_2", DT), ("g_mlp_2", DT), ("g_final_2", DT)):
        VEC[name] = (at, n)
        at += n
    return at


NVEC = _vec_layout()


def unit_blocks(n_k, tiles):
    step = UNIT // (P * tiles)
    return [(k, min(step, n_k - k)) for k in range(0, n_k, step)]


def ffn_pieces(n_hidden):
    half = (n_hidden // 2 + 1) // 2 * 2
    return [(0, half), (half, n_hidden - half)]


def swiglu_groups(first, count):
    out = []
    for j in range(first, first + count, 2):
        out += [[j, j + 1], [FF // P + j, FF // P + j + 1]]
    return out


def pairs(first, count):
    return [[j, j + 1] for j in range(first, first + count, 2)]


class Step:

    def __init__(self, lane, fn, after, sem, by):
        self.lane, self.fn, self.after, self.sem, self.by = lane, fn, after, sem, by
        self.used, self.value = False, None


def flat(x):
    if x is None:
        return
    if isinstance(x, (list, tuple)):
        for y in x:
            yield from flat(y)
    else:
        yield x


class Lane:

    def __init__(self, sem):
        self.sem, self.items = sem, []

    def do(self, fn, after=(), place=None, sem=None, by=1):
        after = list(flat(after))
        for s in after:
            s.used = True
        step = Step(self, fn, after, self.sem if sem is None else sem, by)
        (self.items if place is None else place).append(step)
        return step

    def place(self):
        self.items.append([])
        return self.items[-1]

    def steps(self):
        return list(flat(self.items))


def count(lanes):
    totals = {}
    for lane in lanes:
        for s in lane.steps():
            if s.used or s.by == 16:
                totals[id(s.sem)] = totals.get(id(s.sem), 0) + s.by
                s.value = totals[id(s.sem)]


def emit(lane, eng):
    seen = {}
    for s in lane.steps():
        need = {}
        for a in s.after:
            k = id(a.sem)
            if a.value > seen.get(k, 0) and a.value > need.get(k, (None, 0))[1]:
                need[k] = (a.sem, a.value)
        for k, (sem, value) in need.items():
            eng.wait_ge(sem, value)
            seen[k] = value
        ins = s.fn(eng)
        if s.value is not None:
            ins.then_inc(s.sem, s.by)


class Buf:

    def __init__(self, ap):
        self.ap, self.free, self.ready = ap, [], []


class Ring:
    def __init__(self, bufs):
        self.bufs, self.n = bufs, 0

    def take(self):
        self.n += 1
        return self.bufs[(self.n - 1) % len(self.bufs)]


class Pair:

    def __init__(self, hi, lo):
        self.hi, self.lo, self.ready, self.used = hi, lo, {}, []


def tiles(t):
    return [t[:, j, :] for j in range(t.shape[1])]


def build(nc, x_in, vec_in, ident_in, tri_in, decay_in, rope_in, sel_in, mem_in, onehot_in, band_in, table_in,
          rg_in, w, out):
    ctx = ExitStack()
    with ctx:
        def sb(name, shape, dt=F32):
            return ctx.enter_context(nc.sbuf_tensor(name, shape, dt))

        def overlay(*plans):
            out, most = {}, 0
            for plan in plans:
                size = 0
                with ExitStack() as inner:
                    for name, shape, dt in plan:
                        out[name] = inner.enter_context(nc.sbuf_tensor(name, shape, dt))
                        size += int(np.prod(shape[1:]))
                most = max(most, size)
            ctx.enter_context(nc.sbuf_tensor(f"{plans[0][0][0]}_room", [P, most], F32))
            return out

        def sem(name):
            return ctx.enter_context(nc.semaphore(name))

        pe, act, dve, pool, sp = lanes = [Lane(sem(n)) for n in
                                          ("pe_done", "act_done", "dve_done", "pool_done", "sp_done")]
        raw_sem = [sem(f"unit_loaded_{i}") for i in range(RAW)]
        const_sem, bias_sem, out_sem = sem("constants_loaded"), sem("bias_moved"), sem("output_stored")
        rg_sem = [sem(f"recurrence_weights_loaded_{i}") for i in range(2)]
        tile_sem = [sem(f"bias_tile_loaded_{i}") for i in range(2)]


        xT_sb = sb("xT", [P, DT, S])
        in_hi, in_lo = sb("in_hi", [P, DT, S], F32R), sb("in_lo", [P, DT, S], F32R)
        raw = sb("raw", [P, RAW, UNIT])
        w_hi, w_lo = sb("w_hi", [P, SPLIT, UNIT], F32R), sb("w_lo", [P, SPLIT, UNIT], F32R)
        vec = sb("vec", [P, NVEC])
        ident, ones, ident_r = sb("ident", [P, P]), sb("ones", [P, P]), sb("ident_r", [P, P], F32R)
        small = overlay([("ssum", [P, S], F32), ("tri", [P, P], F32)],
                        [("forget_parts", [P, S], F32R), ("tri_r", [P, P], F32R)])
        rstd_sb, ssum_sb, tri, tri_r = sb("rstd_b", [P, S]), small["ssum"], small["tri"], small["tri_r"]
        stat_sb = sb("stat", [P, 8, 8])
        soft_sb = sb("soft", [P, 4, 4])
        col_sb = sb("col", [P, 3, 8])
        lruv = sb("lruv", [P, 11, DT])
        table_sb = sb("rel_table", [P, 3 * GH])
        halfb = sb("halfb", [P, 3 * DT])
        NTMP = 5
        tmp_sb = sb("tmp", [P, NTMP, S])

        HID = 16
        f, r = F32, F32R
        m = overlay(
            [("hid_hi", [P, HID, S], r), ("hid_lo", [P, HID, S], r), ("silu", [P, 4, S], f),
             ("gained_ssum", [P, S], f), ("gap_9", [P, 9, S], f), ("final_rstd", [P, S], f)],
            [("gap_0", [P, 36, S], f), ("onehot", [P, 3, 2 * S], f), ("rel", [P, 3, 2 * S], f)],
            [("fq", [P, 4, S], f), ("fk", [P, 4, S], f), ("rq", [P, RH, S], f), ("rk", [P, RH, S], f),
             ("fv", [P, TT, S], f), ("rv", [P, TT, S], f), ("gate", [P, 2 * DT, S], f),
             ("srg", [P, RH, S], f), ("decay", [P, RH, S], f), ("p_1", [P, 2, S], f),
             ("pt_1", [P, 2, S], f), ("negc", [P, S], f)],
            [("fox_hi", [P, 4, S], r), ("fox_lo", [P, 4, S], r), ("ret_hi", [P, RH, S], r),
             ("ret_lo", [P, RH, S], r), ("gap_1", [P, 16, S], f), ("sel", [P, FH * P], f),
             ("rope", [P, 4, S], f)],
            [("gap_2", [P, 32, S], f), ("sel_r", [P, FH * P], r)],
            [("dq", [P, 6, S], f), ("dk", [P, 6, S], f), ("lru_hi", [P, RT, S], r),
             ("lru_lo", [P, RT, S], r), ("mq", [P, MH, S], f), ("dv", [P, TT, 3, GH * GD], f),
             ("mk", [P, MH, NMEM], f), ("mv", [P, 2, MH * P], f), ("p_2", [P, 2, 768], f),
             ("pt_2", [P, 768], f), ("bias", [P, 2, 768], f), ("dil_hi", [P, 2, S], r),
             ("dil_lo", [P, 2, S], r), ("pad", [P, S + 4], f), ("rgw", [P, 2, 2 * P], f)],
            [("gap_7", [P, 12, S], f), ("lru_x", [P, RT, S], f), ("lru_g", [P, RT, S], f)],
            [("acc", [P, DT, S], f), ("memo_lo", [P, MH, S], r), ("mrg2_hi", [P, DT, S], r),
             ("mrg2_lo", [P, DT, S], r), ("memo_hi", [P, MH, S], r), ("gate2", [P, DT, S], f)],
            [("gap_5", [P, 16, S], f), ("mrg_hi", [P, DT, S], r), ("gap_6", [P, 16, S], f),
             ("mrg_lo_a", [P, 4, S], r), ("gap_8", [P, 4, S], f), ("mrg_lo_b", [P, 4, S], r)],
            [("gap_4", [P, 38, S], f), ("mem_hi", [P, DT, NMEM], r), ("mem_lo", [P, DT, NMEM], r),
             ("memx", [P, DT, NMEM], f), ("mem_rstd", [P, NMEM], f), ("mem_ssum", [P, NMEM], f)])

        bank = [Buf(ctx.enter_context(nc.psum_tensor(f"bank_{i}", [P, S], F32))[:]) for i in range(4)]
        score_ps = ctx.enter_context(nc.psum_tensor("score_ps", [P, 2 * S], F32))
        score = [Buf(score_ps[:, i * S:(i + 1) * S]) for i in range(2)]
        turn = Buf(ctx.enter_context(nc.psum_tensor("turn_ps", [P, S], F32))[:])
        outp = Buf(ctx.enter_context(nc.psum_tensor("out_ps", [P, S], F32))[:])

        def load(dst, src, sem, after=(), place=None):
            return sp.do(lambda e: e.dma_start(dst, src), after, place=place, sem=sem, by=16)

        vec_loaded = load(vec[:], vec_in, sem("vectors_loaded"))
        x_loads, first_places = [], []
        for i in range(DT // 2):
            first_places.append(sp.place())
            x_loads.append(load(xT_sb[:, 2 * i:2 * i + 2, :], x_in[:, 2 * i:2 * i + 2, :], sem(f"input_loaded_{i}")))
        const_loads = [load(ident[:], ident_in, const_sem), load(tri[:], tri_in, const_sem)]
        mask_parts = []
        ones_set = dve.do(lambda e: e.memset(ones[:], 1.0))

        def col(name, j, rows=P):
            return vec[0:rows, VEC[name][0] + j:VEC[name][0] + j + 1]

        tmp = Ring([Buf(tmp_sb[:, i, :]) for i in range(NTMP)])
        xT = [Buf(xT_sb[:, j, :]) for j in range(DT)]
        for j in range(DT):
            xT[j].ready = [x_loads[j // 2], vec_loaded]

        class Units:
            n = 0
            places, load_places = [], []
            hi, lo, used = [], [], []
            cursor = {name: 0 for name in w}

        def next_unit(name, cols):
            i = Units.n
            Units.n += 1
            rs, ss = i % RAW, i % SPLIT
            at = Units.cursor[name]
            Units.cursor[name] += P * cols
            src = w[name][at:at + P * cols].rearrange("(p n) -> p n", p=P)
            loaded = load(raw[:, rs, 0:cols], src, raw_sem[rs],
                          [Units.hi[i - RAW], Units.lo[i - RAW]] if i >= RAW else [], place=Units.load_places[i])
            freed = [Units.used[i - SPLIT]] if i >= SPLIT else []
            a_place, d_place = Units.places[i]
            wr, wh, wl = raw[:, rs, 0:cols], w_hi[:, ss, 0:cols], w_lo[:, ss, 0:cols]
            hi = act.do(lambda e: e.activation(wh, wr, ACT.Copy), [loaded, freed], place=a_place)
            lo = dve.do(lambda e: e.tensor_tensor(wl, wr, wh.bitcast(F32), ALU.subtract),
                        [loaded, hi, freed], place=d_place)
            Units.hi.append(hi)
            Units.lo.append(lo)
            return wh, wl, [hi, lo]

        filler = deque()
        hooks = deque()
        late_hooks = deque()
        rate, due = [1], [0]
        waiting = []

        put = [None]
        soon = []

        def put_off(fn):
            if put[0] is None:
                fn()
            else:
                put[0].append(fn)

        def run_soon():
            now, soon[:] = list(soon), []
            for fn in now:
                fn()

        def drain():
            while filler:
                filler.popleft()()

        def flush():
            run_soon()
            while waiting:
                waiting.pop(0)()

        class Groups:
            n = 0

        def gemm(name, n_k, groups, src, evict, first_k=0, n=S, rows=None):
            for group in groups:
                banks = [bank[2 * (Groups.n % 2) + i] for i in range(2)]
                Groups.n += 1
                nt = len(group)
                if rows is None:
                    outs = [(banks[m], banks[m].ap[:, 0:n]) for m in range(nt)]
                else:
                    outs = [(banks[t // 2], banks[t // 2].ap[:, (t % 2) * 256:(t % 2) * 256 + 256])
                            for t in range(len(rows))]
                done = [None] * len(outs)
                for k0, nk in unit_blocks(n_k, nt):
                    wh, wl, w_ready = next_unit(name, nk * nt * P)
                    if any(first_k + k0 + k not in src.ready for k in range(nk)):
                        flush()
                    wh3 = wh.rearrange("p (k c) -> p k c", k=nk)
                    wl3 = wl.rearrange("p (k c) -> p k c", k=nk)
                    pops, at, total = 0, 0, len(outs) * nk
                    due[0] += rate[0]
                    n_pops = int(due[0])
                    due[0] -= n_pops
                    for o, (b, ps) in enumerate(outs):
                        for k in range(nk):
                            kk = first_k + k0 + k
                            after = [src.ready[kk], w_ready, b.free if k0 + k == 0 else []]
                            first = k0 + k == 0 and (rows is None or o % 2 == 0)
                            last = k0 + k == n_k - 1
                            for step, (xa, wa) in enumerate(((src.hi, wh3), (src.lo, wh3), (src.hi, wl3))):
                                if rows is None:
                                    lhs, rhs = wa[:, k, o * P:(o + 1) * P], xa[kk]
                                else:
                                    lhs, rhs = rows[o](xa[kk]), wa[:, k, :]
                                done[o] = pe.do(
                                    lambda e, ps=ps, lhs=lhs, rhs=rhs, st=first and step == 0, sp_=last and step == 2:
                                    e.matmul(ps, lhs, rhs, start=st, stop=sp_, skip_group_check=True),
                                    after if step == 0 else [])
                            at += 1
                            while pops < n_pops and at < total and at >= (pops + 1) * total // (n_pops + 1):
                                pops += 1
                                if filler:
                                    filler.popleft()()
                    Units.used.append(done[-1])
                    src.used = [done[-1]]
                    Units.places.append((act.place(), dve.place()))
                    Units.load_places.append(sp.place())
                    if hooks:
                        hooks.popleft()()
                    flush()
                    if late_hooks:
                        late_hooks.popleft()()

                def evict_group(group=group, outs=outs, done=list(done), banks=banks):
                    frees = {id(b): [] for b in banks}
                    put[0] = late = []
                    for o, (b, ps) in enumerate(outs):
                        which, last = (group[o], done[o]) if rows is None else ((group, o), done[-1])
                        frees[id(b)].append(evict(which, ps, last))
                    for b in banks:
                        b.free = frees[id(b)]
                    put[0] = None
                    for fn in late:
                        fn()

                waiting.append(evict_group)

        def split(x_ap, x_ready, dst, j, scale=None, scale_ready=()):
            hi_ap, lo_ap = dst.hi[j], dst.lo[j]
            used = list(flat(dst.used))
            if scale is None:
                hi = act.do(lambda e: e.activation(hi_ap, x_ap, ACT.Copy), [x_ready, used])
            else:
                hi = act.do(lambda e: e.activation(hi_ap, x_ap, ACT.Copy, scale=scale), [x_ready, used, scale_ready])
            steps = [hi]

            def low():
                if scale is None:
                    lo = dve.do(lambda e: e.tensor_tensor(lo_ap, x_ap, hi_ap.bitcast(F32), ALU.subtract),
                                [x_ready, hi, used])
                else:
                    lo = dve.do(lambda e: e.scalar_tensor_tensor(lo_ap, x_ap, scale, hi_ap.bitcast(F32),
                                                                 ALU.mult, ALU.subtract), [x_ready, hi, used])
                steps.append(lo)
                dst.ready[j] = steps
            put_off(low)
            return steps

        inp = Pair(tiles(in_hi), tiles(in_lo))

        def square_sum(x_ap, ready, j, ssum, scale=1.0):
            if j == 0:
                ssum.ready = [act.do(lambda e: e.activation(ssum.ap, x_ap, ACT.Square, scale=scale),
                                     [ready, ssum.free])]
                return ssum.ready
            t = tmp.take()
            n = ssum.ap.shape[1]
            sq = act.do(lambda e: e.activation(t.ap[:, 0:n], x_ap, ACT.Square, scale=scale), [ready, t.free])
            add = pool.do(lambda e: e.tensor_tensor(ssum.ap, ssum.ap, t.ap[:, 0:n], ALU.add), [sq, ssum.ready])
            t.free, ssum.ready = [add], [add]
            return [sq]

        def norm_tile(j, gain, ssum, gain_at=0):
            if j == 0:
                inp.ready = {}
            x = xT[j]
            x.free = [split(x.ap, x.ready, inp, j, scale=col(gain, gain_at + j)), square_sum(x.ap, x.ready, j, ssum)]

        stat_free = [[]]

        def rsqrt(v_ap, ready, n, over, dst):
            c = [stat_sb[:, i, 0:n] for i in range(8)]
            last = dve.do(lambda e: e.tensor_scalar(c[0], v_ap, 1.0 / over, EPS, ALU.mult, ALU.add),
                          [ready, stat_free[0]])
            read = last
            last = dve.do(lambda e: e.tensor_scalar(c[1].bitcast(I32), c[0].bitcast(I32), 1, None,
                                                    ALU.logical_shift_right), last)
            last = dve.do(lambda e: e.tensor_scalar(c[2].bitcast(I32), c[1].bitcast(I32), -1, 0x5F3759DF,
                                                    ALU.mult, ALU.add), last)
            y = 2
            for it in range(4):
                z = 5 if y == 2 else 2
                to = dst.ap[:, 0:n] if it == 3 else c[z]
                last = dve.do(lambda e, y=y: e.tensor_tensor(c[3], c[y], c[y], ALU.mult), last)
                last = dve.do(lambda e: e.scalar_tensor_tensor(c[4], c[3], -0.5, c[0], ALU.mult, ALU.mult), last)
                last = dve.do(lambda e, y=y, to=to: e.scalar_tensor_tensor(to, c[4], 1.5, c[y], ALU.add, ALU.mult),
                              [last, dst.free if it == 3 else []])
                y = z
            dst.ready = [last]
            stat_free[0] = [last]
            return read

        tok_tiles = [lambda ap, t=t: ap[:, t * P:(t + 1) * P] for t in range(TT)]
        res_tiles = [lambda ap, r=r: ap[:, r::DIL] for r in range(DIL)]

        def stats(ssum, dst, tok, over=D):
            for i, tile in enumerate(tok):
                got = pe.do(lambda e, i=i, tile=tile: e.matmul(turn.ap[:, i:i + 1], tile(ssum.ap), ones[:, 0:1],
                                                               start=True, stop=True, skip_group_check=True),
                            [ssum.ready, ones_set, turn.free])
            ssum.free = [got]
            turn.free = [rsqrt(turn.ap[:, 0:len(tok)], got, len(tok), over, dst)]

        def spread(cols, dst, half=False):
            n = dst.ap.shape[1]
            t = tmp.take()
            for i in range(n // P):
                dg = dve.do(lambda e, i=i: e.tensor_scalar(t.ap[:, i * P:(i + 1) * P], ident[:],
                                                           cols.ap[:, i:i + 1], 0.5 if half else 1.0,
                                                           ALU.mult, ALU.mult),
                            [cols.ready, t.free, const_loads])
            for i in range(n // P):
                got = pe.do(lambda e, i=i: e.matmul(turn.ap[:, i * P:(i + 1) * P], ones[:],
                                                    t.ap[:, i * P:(i + 1) * P], start=True, stop=True,
                                                    skip_group_check=True),
                            [dg, turn.free])
            t.free = [got]
            copied = act.do(lambda e: e.activation(dst.ap, turn.ap[:, 0:n], ACT.Copy), [got, dst.free])
            turn.free = [copied]
            dst.ready, cols.free = [copied], [dg]

        ssum, rstd = Buf(ssum_sb[:]), Buf(rstd_sb[:])
        rcol, hcol, mcol = [Buf(col_sb[:, i, :]) for i in range(3)]

        def norm_hooks(ssum_, cols, dst, tok=tok_tiles, over=D):
            hooks.extend([lambda: None, lambda: stats(ssum_, cols, tok, over),
                          lambda: spread(cols, dst)])

        def times_rstd(dst_ap, ps, done, free=()):
            step = dve.do(lambda e: e.tensor_tensor(dst_ap, ps, rstd.ap, ALU.mult), [done, rstd.ready, free])
            rstd.free = [step]
            return step

        def add_residual(j, ps, done, scale):
            x = xT[j]
            step = dve.do(lambda e: e.scalar_tensor_tensor(x.ap, ps, scale, x.ap, ALU.mult, ALU.add),
                          [done, x.ready, x.free])
            x.ready, x.free = [step], []
            return step

        hid = Pair(tiles(m["hid_hi"]), tiles(m["hid_lo"]))
        silu = Ring([Buf(t) for t in tiles(m["silu"])])

        def feed_forward(w_in, w_out, n_hidden, gated, scale, after_tile):
            for first, n in ffn_pieces(n_hidden):
                held = {}

                def evict_gated(tile, ps, done, first=first, held=held):
                    if tile < n_hidden:
                        b = silu.take()
                        a = times_rstd(b.ap, ps, done, b.free)
                        b.ready = [act.do(lambda e: e.activation(b.ap, b.ap, ACT.Silu), a)]
                        held[tile] = b
                        return a
                    b = held[tile - n_hidden]
                    t = tmp.take()
                    up = times_rstd(t.ap, ps, done, t.free)
                    g = dve.do(lambda e: e.tensor_tensor(t.ap, t.ap, b.ap, ALU.mult), [up, b.ready])
                    b.free = [g]
                    t.free = split(t.ap, g, hid, tile - n_hidden - first)
                    return up

                def evict_square(tile, ps, done, first=first):
                    t = tmp.take()
                    a = times_rstd(t.ap, ps, done, t.free)
                    g = dve.do(lambda e: e.scalar_tensor_tensor(t.ap, t.ap, 0.0, t.ap, ALU.max, ALU.mult), a)
                    t.free = split(t.ap, g, hid, tile - first)
                    return a

                def evict_out(j, ps, done, last=first + n == n_hidden):
                    step = add_residual(j, ps, done, scale)
                    if last:
                        after_tile(j)
                    return step

                hid.ready = {}
                gemm(w_in, DT, swiglu_groups(first, n) if gated else pairs(first, n), inp,
                     evict_gated if gated else evict_square)
                gemm(w_out, n, pairs(0, DT), hid, evict_out)

        soft = Ring([Buf(soft_sb[:, i, :]) for i in range(4)])

        def softmax_rest(p, width, src_ap, exp_scale, top, top_scale, c):
            neg = dve.do(lambda e: e.tensor_scalar(c.ap[:, 1:2], c.ap[:, 0:1], top_scale, None, ALU.mult), top)
            pw = p.ap[:, 0:width]
            ex = act.do(lambda e: e.activation(pw, src_ap, ACT.Exp, bias=c.ap[:, 1:2], scale=exp_scale,
                                               accum_out=c.ap[:, 2:3]), [neg, p.free])
            inv = dve.do(lambda e: e.reciprocal(c.ap[:, 3:4], c.ap[:, 2:3]), ex)
            got = dve.do(lambda e: e.tensor_scalar(pw, pw, c.ap[:, 3:4], None, ALU.mult), inv)
            c.free = [got]
            p.ready = [got]
            return ex

        def softmax_biased(p, width, ps_ap, bias_ap, ready):
            c = soft.take()
            pw = p.ap[:, 0:width]
            top = dve.do(lambda e: e.tensor_tensor_reduce(pw, ps_ap, bias_ap, FDH ** -0.5, LOWEST, ALU.add,
                                                          ALU.max, c.ap[:, 0:1]),
                         [ready, p.free, c.free])
            softmax_rest(p, width, pw, 1.0, top, -1.0, c)
            return top

        def turn_p(p, blocks, pt, turn_, at=0):
            for b in range(blocks):
                t = pe.do(lambda e, b=b: e.transpose(turn_.ap[:, b * P:(b + 1) * P],
                                                     p.ap[:, at + b * P:at + (b + 1) * P], ident[:]),
                          [p.ready, turn_.free])
            cp = act.do(lambda e: e.activation(pt.ap[:, at:at + blocks * P], turn_.ap[:, 0:blocks * P], ACT.Copy),
                        [t, pt.free])
            turn_.free = [cp]
            return t, cp

        fq, fk, rq, rk, srg, gate = [tiles(m[n]) for n in ("fq", "fk", "rq", "rk", "srg", "gate")]
        fv, rv, decay, rope, sel, sel_r = [m[n] for n in ("fv", "rv", "decay", "rope", "sel", "sel_r")]
        forget_parts = small["forget_parts"]
        p1, pt1 = [Ring([Buf(t) for t in tiles(m[n])]) for n in ("p_1", "pt_1")]
        negc = Buf(m["negc"][:])
        decay_sem, decay_loaded = sem("decay_loaded"), []
        table_sem = sem("mixing_tables_loaded")

        def mixing1(l):
            fox = Pair(tiles(m["fox_hi"]), tiles(m["fox_lo"]))
            ret = Pair(tiles(m["ret_hi"]), tiles(m["ret_lo"]))
            mrg = Pair(tiles(m["mrg_hi"]), tiles(m["mrg_lo_a"]) + tiles(m["mrg_lo_b"]))
            ready = {}
            if l == 0:
                decay_loaded.append(load(decay[:], decay_in, decay_sem, bias_stores))
            tables = [load(rope[:], rope_in, table_sem, [region_free, silu_free()]),
                      load(sel[0:PARTS, :], sel_in, table_sem, [region_free, silu_free()])]

            def evict_q(dst, key):
                def evict(j, ps, done):
                    ready[key, j] = times_rstd(dst[j], ps, done)
                    return ready[key, j]
                return evict

            def evict_v(dst, key, tok_cols=0):
                def evict(which, ps, done):
                    group, t = which
                    at = group[0] * P
                    step = act.do(lambda e: e.activation(dst[:, t, at:at + 256], ps, ACT.Copy,
                                                         scale=rcol.ap[:, t:t + 1]), [done, rcol.ready])
                    ready[key, t, group[0]] = step
                    rcol.free = [rcol.free, step]
                    return step
                return evict

            def evict_f(j, ps, done):
                f = tmp.take()
                a = tmp.take()
                fa, aa = f.ap[0:FH, :], a.ap[0:FH, :]
                x = dve.do(lambda e: e.tensor_tensor(fa, ps[0:FH, :], rstd.ap[0:FH, :], ALU.mult),
                           [done, rstd.ready, f.free])
                x2 = dve.do(lambda e: e.tensor_scalar(fa, fa, col("b_forget", l, FH), None, ALU.add), x)
                ab = dve.do(lambda e: e.scalar_tensor_tensor(aa, fa, -1.0, fa, ALU.mult, ALU.max), [x2, a.free])
                ex = act.do(lambda e: e.activation(aa, aa, ACT.Exp, scale=-1.0), ab)
                ln = act.do(lambda e: e.activation(aa, aa, ACT.Ln, bias=1.0), ex)
                sp_ = dve.do(lambda e: e.scalar_tensor_tensor(aa, fa, 0.0, aa, ALU.min, ALU.subtract), ln)
                ng = dve.do(lambda e: e.tensor_scalar(aa, aa, -1.0, None, ALU.mult), sp_)
                sc = dve.do(lambda e: e.tensor_tensor_scan(fa, aa, aa, 0.0, ALU.add, ALU.max), ng)
                hi_rows, lo_rows = forget_parts[0:FH, :], forget_parts[32:PARTS, :]
                zero = act.do(lambda e: e.activation(forget_parts[0:PARTS, :], rstd.ap[0:PARTS, :], ACT.Copy, scale=0.0),
                              [ssum.free, rstd.ready])
                hi = act.do(lambda e: e.activation(hi_rows, fa, ACT.Copy), [sc, zero])
                lo = dve.do(lambda e: e.tensor_tensor(lo_rows, fa, hi_rows.bitcast(F32), ALU.subtract), [hi, sc])
                selectors = act.do(lambda e: e.activation(sel_r[0:PARTS, :], sel[0:PARTS, :], ACT.Copy), tables)
                rstd.free = [rstd.free, zero]
                f.free, a.free = [lo], [sc]
                ready["c"] = [lo, selectors]
                return x

            def evict_rope(dst, key, table):
                def evict(j, ps, done):
                    t, u = tmp.take(), tmp.take()
                    x = times_rstd(t.ap, ps, done, t.free)
                    s1 = act.do(lambda e: e.activation(u.ap[0:64, :], t.ap[64:128, :], ACT.Copy), [x, u.free])
                    s2 = act.do(lambda e: e.activation(u.ap[64:128, :], t.ap[0:64, :], ACT.Copy), [x, u.free])
                    c = pool.do(lambda e: e.tensor_tensor(t.ap, t.ap, rope[:, table, :], ALU.mult), [s2, tables])
                    d = pool.do(lambda e: e.tensor_tensor(u.ap, u.ap, rope[:, table + 1, :], ALU.mult), [s2, tables])

                    def add():
                        ready[key, j] = dve.do(lambda e: e.tensor_tensor(dst[j], t.ap, u.ap, ALU.add), [c, d])
                        t.free = u.free = [ready[key, j]]
                    soon.append(add)
                    return x
                return evict

            def evict_rg(j, ps, done):
                t, u = tmp.take(), tmp.take()
                x = times_rstd(t.ap, ps, done, t.free)
                th = act.do(lambda e: e.activation(u.ap, t.ap, ACT.Tanh, scale=0.5), [x, u.free])

                def product():
                    ready["srg", j] = dve.do(lambda e: e.scalar_tensor_tensor(srg[j], u.ap, 1.0, t.ap,
                                                                              ALU.add, ALU.mult), th)
                    t.free = u.free = [ready["srg", j]]
                put_off(product)
                return x

            def evict_gate(j, ps, done):
                t = tmp.take()
                x = times_rstd(t.ap, ps, done, t.free)
                ready["gate", j] = act.do(lambda e: e.activation(gate[j], t.ap, ACT.Tanh, scale=0.5),
                                          [x, tables_used])
                t.free = [ready["gate", j]]
                return x

            tables_used = []

            state = {}

            def fox_scores(n):
                h, i = divmod(n, TT)
                base, j, keys = 64 * (h % 2), h // 2, (i + 1) * P
                if i == 0:
                    b = pe.do(lambda e: e.matmul(turn.ap, sel_r[0:PARTS, h * P:(h + 1) * P],
                                                 forget_parts[0:PARTS, :], start=True, stop=True),
                              [ready["c"], turn.free])
                    ssum.free = [b]
                    negc.ready = [act.do(lambda e: e.activation(negc.ap, turn.ap, ACT.Copy, scale=FDH ** 0.5),
                                         [b, negc.free])]
                    turn.free = negc.ready
                sc, p = score[n % 2], p1.take()
                qk = pe.do(lambda e: e.matmul(sc.ap[:, 0:keys], fq[j][base:base + 64, i * P:(i + 1) * P],
                                              fk[j][base:base + 64, 0:keys], start=True, stop=False,
                                              skip_group_check=True),
                           [ready["fq", j], ready["fk", j], sc.free])
                mk = pe.do(lambda e: e.matmul(sc.ap[:, i * P:keys], ident_r[:], tri_r[:], start=False,
                                              stop=True, skip_group_check=True), mask_parts)
                top = softmax_biased(p, keys, sc.ap[:, 0:keys], negc.ap[:, 0:keys], [mk, negc.ready])
                sc.free, negc.free = [top], [top]
                state[n] = p

            def fox_turn(n):
                h, i = divmod(n, TT)
                p, pt = state[n], pt1.take()
                t, cp = turn_p(p, i + 1, pt, turn)
                p.free, pt.ready = [t], [cp]
                state[n] = pt

            def fox_values(n):
                h, i = divmod(n, TT)
                base, j, pt = 64 * (h % 2), h // 2, state.pop(n)
                for b in range(i + 1):
                    g = pe.do(lambda e, b=b: e.matmul(outp.ap[base:base + 64, i * P:(i + 1) * P],
                                                      fv[:, b, h * FDH:(h + 1) * FDH],
                                                      pt.ap[:, b * P:(b + 1) * P], start=b == 0, stop=b == i,
                                                      skip_group_check=True),
                              [pt.ready, ready["fv", b, h // 4 * 2], outp.free])
                pt.free = [g]
                if h % 2 and i == TT - 1:
                    outp.free = split(outp.ap, g, fox, j)

            def ret_scores(n):
                h, i = divmod(n, TT)
                w_, p, sc = S - i * P, p1.take(), score[n % 2]
                qk = pe.do(lambda e: e.matmul(sc.ap[:, 0:w_], rk[h][:, i * P:(i + 1) * P], rq[h][:, i * P:S],
                                              start=True, stop=True, skip_group_check=True),
                           [ready["rq", h], ready["rk", h], sc.free])
                p.ready = [dve.do(lambda e: e.tensor_tensor(p.ap[:, 0:w_], sc.ap[:, 0:w_], decay[:, h, 0:w_],
                                                            ALU.mult), [qk, p.free, decay_loaded])]
                sc.free = p.ready
                state["r", n] = p

            def ret_values(n):
                h, i = divmod(n, TT)
                w_, p = S - i * P, state.pop(("r", n))
                g = pe.do(lambda e: e.matmul(outp.ap[:, i * P:S], rv[:, i, h * P:(h + 1) * P], p.ap[:, 0:w_],
                                             start=i == 0, stop=i == TT - 1, skip_group_check=True),
                          [p.ready, ready["rv", i, h // 2 * 2], outp.free])
                p.free = [g]
                if i == TT - 1:
                    o, sq = pt1.take(), pt1.take()
                    c1 = act.do(lambda e: e.activation(sq.ap, outp.ap, ACT.Square), [g, sq.free])
                    c2 = act.do(lambda e: e.activation(o.ap, outp.ap, ACT.Copy), [g, o.free])
                    outp.free = [c2]
                    sq.ready, sq.free, o.ready, o.free = [c1], [], [c2], []
                    state["o", h] = o, sq

            def ret_stats(h):
                stats(state["o", h][1], hcol, tok_tiles, P)

            def ret_finish(h):
                o, _ = state.pop(("o", h))
                b = Buf(tmp.take().ap)
                tb = tmp.bufs[(tmp.n - 1) % NTMP]
                b.free = tb.free
                spread(hcol, b, half=True)
                g = pool.do(lambda e: e.tensor_tensor(o.ap, o.ap, srg[h], ALU.mult), [o.ready, ready["srg", h]])
                y = dve.do(lambda e: e.scalar_tensor_tensor(b.ap, o.ap, col("ret_norm", RH * l + h), b.ap,
                                                            ALU.mult, ALU.mult), [g, b.ready])
                o.free = [y]
                tb.free = split(b.ap, y, ret, h)

            def chain(n_steps, *stages_):
                for n in range(n_steps + len(stages_) - 1):
                    def slot(n=n):
                        for k, stage in enumerate(stages_):
                            if 0 <= n - k < n_steps:
                                stage(n - k)
                    filler.append(slot)

            name = f"mix{l}"
            norm_hooks(ssum, rcol, rstd)
            rate[0] = 0
            gemm(name, DT, pairs(0, 4), inp, evict_q(fq, "fq"))
            gemm(name, DT, [[0]], inp, evict_f)
            gemm(name, DT, pairs(0, 4), inp, evict_q(fk, "fk"))
            gemm(name, DT, pairs(0, 4), inp, evict_v(fv, "fv"), rows=tok_tiles)
            flush()
            for n in range(FH * TT + 2):
                def fox_slot(n=n):
                    if n < FH * TT:
                        fox_scores(n)
                    if n >= 2:
                        fox_values(n - 2)
                    if 0 <= n - 1 < FH * TT:
                        fox_turn(n - 1)
                filler.append(fox_slot)

            def ret_end(n):
                if n % TT == TT - 1:
                    ret_stats(n // TT)

            def ret_end2(n):
                if n % TT == TT - 1:
                    ret_finish(n // TT)
            chain(RH * TT, ret_scores, ret_values, ret_end, ret_end2)
            rate[0] = 2
            gemm(name, DT, pairs(0, RH), inp, evict_rope(rq, "rq", 0))
            gemm(name, DT, pairs(0, RH), inp, evict_rope(rk, "rk", 2))
            gemm(name, DT, pairs(0, 4), inp, evict_v(rv, "rv"), rows=tok_tiles)
            gemm(name, DT, pairs(0, RH), inp, evict_rg)
            tables_used += [ready["rk", RH - 1]]
            gemm(name, DT, pairs(0, 2 * DT), inp, evict_gate)
            flush()
            drain()
            rate[0] = 1

            def evict_ret(j, ps, done):
                ready["m", j] = dve.do(lambda e: e.scalar_tensor_tensor(gate[j], gate[j], 1.0, ps, ALU.add, ALU.mult),
                                       [done, ready["gate", j]])
                return ready["m", j]

            def evict_fox(j, ps, done):
                g = gate[DT + j]
                u = dve.do(lambda e: e.scalar_tensor_tensor(g, g, 1.0, ps, ALU.add, ALU.mult),
                           [done, ready["gate", DT + j]])
                s_ = pool.do(lambda e: e.tensor_tensor(gate[j], gate[j], g, ALU.add), [u, ready["m", j]])
                split(gate[j], s_, mrg, j)
                return u

            for j in range(0, DT, 2):
                gemm(f"w_o_ret{l}", RH, [[j, j + 1]], ret, evict_ret)
                gemm(f"w_o_fox{l}", 4, [[j, j + 1]], fox, evict_fox)

            def evict_out(j, ps, done):
                step = add_residual(j, ps, done, 0.5)
                norm_tile(j, "norm_ffn2", ssum, DT * l)
                return step
            gemm(f"w_out{l}", DT, pairs(0, DT), mrg, evict_out)
            region_free[:] = [mrg.used]

        region_free = []

        def silu_free():
            return [b.free for b in silu.bufs]

        scratch = nc.dram_tensor("bias_by_distance", [3 * GH, 2 * S], F32, kind="Internal").ap()
        onehot, rel = m["onehot"], m["rel"]
        bias_loads, bias_stores = [], []

        def load_bias_tables():
            bias_loads.extend([load(onehot[0:NB], onehot_in, bias_sem), load(rel[0:GH], band_in, bias_sem),
                               load(table_sb[0:NB, :], table_in, bias_sem)])

        def bias_by_distance(g):
            for half in range(2):
                b, cut = score[half], slice(half * S, half * S + S)
                t = pe.do(lambda e, b=b, cut=cut: e.matmul(b.ap[0:GH, :], table_sb[0:NB, g * GH:(g + 1) * GH],
                                                           onehot[0:NB, g, cut], start=True, stop=True),
                          [bias_loads, b.free])
                r_ = dve.do(lambda e, b=b, cut=cut: e.scalar_tensor_tensor(
                    rel[0:GH, g, cut], b.ap[0:GH, :], GD ** 0.5, rel[0:GH, g, cut], ALU.mult, ALU.add), [t, bias_loads])
                b.free = [r_]
            bias_stores.append(load(scratch[g * GH:(g + 1) * GH, :], rel[0:GH, g, :], bias_sem, [r_]))

        WIDE, NEAR = 2 * S, 2 * P
        wide = nc.dram_tensor("bias_rows_wide", [GH, P * (WIDE + DIL)], F32, kind="Internal").ap()
        near = nc.dram_tensor("bias_rows_near", [2 * GH, P * (NEAR + 1)], F32, kind="Internal").ap()
        bias_rows = []

        def lay_bias_rows():
            for gh in range(3 * GH):
                if gh < GH:
                    dst = wide[gh, :].rearrange("(j y) -> j y", j=P)[:, 0:WIDE]
                    src = bass.AP(tensor=scratch.tensor, offset=gh * 2 * S, ap=[[0, P], [1, WIDE]])
                else:
                    dst = near[gh - GH, :].rearrange("(j y) -> j y", j=P)[:, 0:NEAR]
                    src = bass.AP(tensor=scratch.tensor, offset=gh * 2 * S + S - P, ap=[[0, P], [1, NEAR]])
                bias_rows.append(load(dst, src, bias_sem, bias_stores))

        lam = vec[:, VEC["lru_lambda_2"][0]:VEC["lru_lambda_2"][0] + RT]
        lv = [lruv[:, i, 0:RT] for i in range(10)]

        both_gains = lruv[:, 10, :]
        fixed = {}

        def small_constants():
            def small_op(fn, after):
                return dve.do(fn, [after, vec_loaded])
            st = small_op(lambda e: e.scalar_tensor_tensor(lv[0], lam, -1.0, lam, ALU.mult, ALU.max), [])
            st = act.do(lambda e: e.activation(lv[1], lv[0], ACT.Exp, scale=-1.0), st)
            st = small_op(lambda e: e.tensor_scalar(lv[2], lv[1], 2.0, None, ALU.add), st)
            st = small_op(lambda e: e.reciprocal(lv[3], lv[2]), st)
            st = small_op(lambda e: e.tensor_tensor(lv[4], lv[1], lv[3], ALU.mult), st)
            st = small_op(lambda e: e.tensor_tensor(lv[5], lv[4], lv[4], ALU.mult), st)
            st = small_op(lambda e: e.tensor_scalar(lv[6], lv[5], 1.0 / 15, None, ALU.mult), st)
            for k in (13, 11, 9, 7, 5, 3):
                st = small_op(lambda e, k=k: e.scalar_tensor_tensor(lv[6], lv[6], 1.0 / k, lv[5], ALU.add, ALU.mult), st)
            st = small_op(lambda e: e.scalar_tensor_tensor(lv[6], lv[6], 1.0, lv[4], ALU.add, ALU.mult), st)
            st = small_op(lambda e: e.tensor_scalar(lv[7], lam, -1.0, 0.0, ALU.mult, ALU.max), st)
            st = small_op(lambda e: e.scalar_tensor_tensor(lv[8], lv[6], 2.0, lv[7], ALU.mult, ALU.add), st)
            st = small_op(lambda e: e.tensor_scalar(lv[9], lv[8], -8.0, None, ALU.mult), st)
            fixed["c8"] = small_op(lambda e: e.tensor_scalar(lv[8], lv[8], 8.0, None, ALU.mult), st)
            bg = VEC["b_gate_2"][0]
            fixed["half"] = small_op(lambda e: e.tensor_scalar(halfb[:], vec[:, bg:bg + 3 * DT], 0.5, None, ALU.mult), [])
            gf, gm = VEC["norm_final"][0], VEC["g_mix_2"][0]
            fixed["gains"] = small_op(lambda e: e.tensor_tensor(both_gains, vec[:, gf:gf + DT], vec[:, gm:gm + DT],
                                                                ALU.mult), [])

        memp = Pair(tiles(m["mem_hi"]), tiles(m["mem_lo"]))
        memx, mem_rstd, mem_ssum = tiles(m["memx"]), Buf(m["mem_rstd"][:]), Buf(m["mem_ssum"][:])
        mem_rows = tok_tiles[:NMEM // P]
        mk, mv = tiles(m["mk"]), m["mv"]
        got = {}

        def prepare_memory(after):
            x = []

            def tile(j):
                split(memx[j], x, memp, j, scale=col("g_mem_2", j))
                square_sum(memx[j], x, j, mem_ssum)
            hooks.append(lambda: x.append(load(m["memx"][:], mem_in, sem("memory_loaded"), after)))
            hooks.extend([lambda: None, lambda: None])
            hooks.extend([lambda j=j: tile(j) for j in range(DT)])
            norm_hooks(mem_ssum, mcol, mem_rstd, mem_rows)

        def memory_keys():
            def evict(j, ps, done):
                got["mk", j] = dve.do(lambda e: e.tensor_tensor(mk[j], ps, mem_rstd.ap, ALU.mult),
                                      [done, mem_rstd.ready])
                return got["mk", j]
            gemm("mem", DT, pairs(0, MH), memp, evict, n=NMEM)

        def memory_values():
            def evict(which, ps, done):
                group, t = which
                at = group[0] * P
                step = act.do(lambda e: e.activation(mv[:, t, at:at + 256], ps, ACT.Copy, scale=mcol.ap[:, t:t + 1]),
                              [done, mcol.ready])
                got["mv", t, group[0]] = step
                return step
            gemm("mem", DT, pairs(0, MH), memp, evict, rows=mem_rows)

        def apply_norm(j, gain, rstd):
            x = xT[j]
            step = dve.do(lambda e: e.scalar_tensor_tensor(x.ap, x.ap, col(gain, j), rstd.ap, ALU.mult, ALU.mult),
                          [x.ready, x.free, rstd.ready])
            rstd.free, x.ready, x.free = [step], [step], []

        def mixing2():
            dq, dk, mq, dv = tiles(m["dq"]), tiles(m["dk"]), tiles(m["mq"]), m["dv"]
            p2 = Ring([Buf(t) for t in tiles(m["p_2"])])
            pt2 = Buf(m["pt_2"][:])
            bias = Ring([Buf(t) for t in tiles(m["bias"])])
            pad, rgw = Buf(m["pad"][:]), Ring([Buf(t) for t in tiles(m["rgw"])])
            lru_x, lru_g = tiles(m["lru_x"]), tiles(m["lru_g"])
            lru = Pair(tiles(m["lru_hi"]), tiles(m["lru_lo"]))
            dil = Pair(tiles(m["dil_hi"]), tiles(m["dil_lo"]))
            memo = Pair(tiles(m["memo_hi"]), tiles(m["memo_lo"]))
            mrg = Pair(tiles(m["mrg2_hi"]), tiles(m["mrg2_lo"]))
            acc, gate2 = tiles(m["acc"]), tiles(m["gate2"])
            ready, state = got, {}

            def evict_q(dst, key):
                def evict(j, ps, done):
                    ready[key, j] = times_rstd(dst[j], ps, done)
                    return ready[key, j]
                return evict

            def evict_dv(g):
                def evict(which, ps, done):
                    t = which[1]
                    c = t if g == 0 else TT + t
                    step = act.do(lambda e: e.activation(dv[:, t, g, :], ps, ACT.Copy, scale=rcol.ap[:, c:c + 1]),
                                  [done, rcol.ready])
                    ready["dv", t, g] = step
                    rcol.free = [rcol.free, step]
                    return step
                return evict

            def head_at(g, h):
                return (g * GH + h) // 2, GD * (h % 2)

            def load_bias(n):
                h, r = divmod(n, DIL)
                b = bias.take()
                b.ready = []
                parts = [(0, wide[h, 0:P * WIDE].rearrange("(j y) -> j y", j=P)[:, S - 1 - r:2 * S - 1 - r])]
                parts += [(S + i * P, near[i * GH + h, 0:P * NEAR].rearrange("(j y) -> j y", j=P)[:, P - 1:2 * P - 1])
                          for i in range(2)]
                for at, src in parts:
                    b.ready.append(load(b.ap[:, at:at + src.shape[1]], src, tile_sem[n % 2], [b.free, bias_rows]))
                state["bias", n] = b

            def dil_scores(n):
                h, r = divmod(n, DIL)
                if n == 0:
                    load_bias(0)
                if n + 1 < GH * DIL:
                    load_bias(n + 1)
                b, p = state.pop(("bias", n)), p2.take()
                for g, (at, width) in enumerate(((0, S), (S, P), (S + P, P))):
                    j, base = head_at(g, h)
                    q = dq[j][base:base + GD, r::DIL]
                    k = dk[j][base:base + GD, :] if g == 0 else dk[j][base:base + GD, r::DIL]
                    qk = pe.do(lambda e, q=q, k=k, at=at, width=width: e.matmul(
                        score_ps[:, at:at + width], q, k, start=True, stop=True, skip_group_check=True),
                        [ready["dq", j], ready["dk", j], score[0].free, score[1].free])
                top = softmax_biased(p, 768, score_ps[:, 0:768], b.ap, [qk, b.ready])
                score[0].free = score[1].free = b.free = [top]
                state[n] = p

            def dil_values(n):
                h, r = divmod(n, DIL)
                base = GD * (h % 2)
                vs = [dv[:, t, 0, h * GD:(h + 1) * GD] for t in range(TT)]
                vs += [dv[:, r, g, h * GD:(h + 1) * GD] for g in (1, 2)]
                for b, v in enumerate(vs):
                    g_ = pe.do(lambda e, b=b, v=v: e.matmul(outp.ap[base:base + GD, r * P:(r + 1) * P], v,
                                                            pt2.ap[:, b * P:(b + 1) * P], start=b == 0,
                                                            stop=b == 5, skip_group_check=True),
                               [pt2.ready, outp.free, [ready["dv", t, 0] for t in range(TT)],
                                ready["dv", r, 1], ready["dv", r, 2]])
                pt2.free = [g_]
                if h % 2 and r == DIL - 1:
                    j = h // 2
                    src = outp.ap.rearrange("p (r j) -> p r j", r=DIL)
                    hi_v = dil.hi[j].rearrange("p (j r) -> p r j", r=DIL)
                    lo_v = dil.lo[j].rearrange("p (j r) -> p r j", r=DIL)
                    hi = act.do(lambda e: e.activation(hi_v, src, ACT.Copy), g_)
                    lo = dve.do(lambda e: e.tensor_tensor(lo_v, src, hi_v.bitcast(F32), ALU.subtract), [g_, hi])
                    dil.ready[j] = outp.free = [hi, lo]

            def turn_first(n, blocks):
                p = state[n]
                t, cp = turn_p(p, blocks, pt2, turn)
                p.free, pt2.ready = [t], [cp]

            def turn_rest(n):
                p = state.pop(n)
                t, cp = turn_p(p, 2, pt2, turn, at=4 * P)
                p.free, pt2.ready = [t], [cp]

            def mem_scores(n):
                h, i = divmod(n, TT)
                sc, p, c = score[n % 2], p2.take(), soft.take()
                ps = sc.ap[:, 0:NMEM]
                qk = pe.do(lambda e: e.matmul(ps, mq[h][:, i * P:(i + 1) * P], mk[h], start=True, stop=True,
                                              skip_group_check=True), [ready["mq", h], ready["mk", h], sc.free])
                top = dve.do(lambda e: e.tensor_reduce(c.ap[:, 0:1], ps, AX.X, ALU.max), [qk, c.free])
                ex = softmax_rest(p, NMEM, ps, P ** -0.5, top, -(P ** -0.5), c)
                sc.free = [top, ex]
                state[n] = p

            def mem_values(n):
                h, i = divmod(n, TT)
                for b in range(2):
                    g_ = pe.do(lambda e, b=b: e.matmul(outp.ap[:, i * P:(i + 1) * P], mv[:, b, h * P:(h + 1) * P],
                                                       pt2.ap[:, b * P:(b + 1) * P], start=b == 0, stop=b == 1,
                                                       skip_group_check=True),
                               [pt2.ready, outp.free, ready["mv", b, h // 2 * 2]])
                pt2.free = [g_]
                if i == TT - 1:
                    ready["mo", h] = act.do(lambda e: e.activation(mq[h], outp.ap, ACT.Copy), g_)
                    outp.free = [ready["mo", h]]
                state["last"] = g_

            pad_zero = dve.do(lambda e: e.memset(pad.ap[:, 0:3], 0.0), region_free)

            def evict_lru(tile, ps, done):
                if tile < RT:
                    j = tile
                    x = times_rstd(pad.ap[:, 3:3 + S], ps, done, [pad.free, pad_zero])
                    y = lru_x[j]

                    def convolution():
                        s_ = dve.do(lambda e: e.tensor_scalar(y, pad.ap[:, 0:S], col("conv_w_2", j),
                                                              col("conv_b_2", j), ALU.mult, ALU.add), x)
                        for k in range(1, 4):
                            s_ = dve.do(lambda e, k=k: e.scalar_tensor_tensor(
                                y, pad.ap[:, k:k + S], col("conv_w_2", RT * k + j), y, ALU.mult, ALU.add), s_)
                        pad.free = [s_]
                        ready["x", j] = s_
                    put_off(convolution)
                    return x
                j = tile - 100
                t = tmp.take()
                a = times_rstd(t.ap, ps, done, t.free)
                ready["g", j] = act.do(lambda e: e.activation(lru_g[j], t.ap, ACT.Gelu_apprx_tanh), a)
                t.free = [ready["g", j]]
                if j:
                    late_hooks.append(lambda: (recur_scan(j - 1), gates_soon(j)))
                else:
                    late_hooks.append(lambda: gates_soon(j))
                late_hooks.append(lambda: recur_factor(j))
                if j == RT - 1:
                    late_hooks.append(lambda: recur_scan(j))
                return a

            def gates_soon(j):
                filler.insert(1, lambda: recur_gates(j))

            def recur_gates(j):
                wb, x = rgw.take(), lru_x[j]
                wl = load(wb.ap, rg_in[j], rg_sem[j % 2], wb.free)
                ps = []
                for k in range(2):
                    sc = score[k]
                    ps.append(pe.do(lambda e, sc=sc, k=k: e.matmul(sc.ap, wb.ap[:, k * P:(k + 1) * P], x,
                                                                   start=True, stop=True),
                                    [wl, ready["x", j], sc.free]))
                wb.free = [ps[1]]
                r_, i_, u, a2 = [tmp.take() for _ in range(4)]
                c8, nc8 = lv[8][:, j:j + 1], lv[9][:, j:j + 1]
                s1 = act.do(lambda e: e.activation(r_.ap, score[0].ap, ACT.Sigmoid, bias=col("b_rg_a_2", j)),
                            [ps[0], r_.free])
                s2 = act.do(lambda e: e.activation(i_.ap, score[1].ap, ACT.Sigmoid, bias=col("b_rg_x_2", j)),
                            [ps[1], i_.free])
                score[0].free, score[1].free = [s1], [s2]
                s3 = act.do(lambda e: e.activation(u.ap, r_.ap, ACT.Tanh, scale=c8), [s1, fixed["c8"], u.free])
                ix = pool.do(lambda e: e.tensor_tensor(i_.ap, i_.ap, x, ALU.mult), [s2])
                s4 = act.do(lambda e: e.activation(r_.ap, r_.ap, ACT.Exp, scale=nc8), [s1, s3, fixed["c8"]])
                s5 = act.do(lambda e: e.activation(a2.ap, r_.ap, ACT.Square), [s4, a2.free])
                state["lru", j] = (r_, i_, u, a2, s3, s4, s5, ix, ps[1])

            def recur_factor(j):
                r_, i_, u, a2, s3, s4, s5, ix, last_ps = state.pop(("lru", j))
                v = dve.do(lambda e: e.scalar_tensor_tensor(u.ap, a2.ap, 1.0, u.ap, ALU.add, ALU.mult), [s5, s3])
                mu = act.do(lambda e: e.activation(u.ap, u.ap, ACT.Sqrt), v)
                b = pool.do(lambda e: e.tensor_tensor(i_.ap, i_.ap, u.ap, ALU.mult), [mu, ix])
                u.free = [b]
                state["lru2", j] = (r_, i_, a2, s4, v, b, ix, last_ps)

            def recur_scan(j):
                r_, i_, a2, s4, v, b, ix, last_ps = state.pop(("lru2", j))
                h = dve.do(lambda e: e.tensor_tensor_scan(a2.ap, r_.ap, i_.ap, 0.0, ALU.mult, ALU.add), [b, s4, v])
                y = dve.do(lambda e: e.tensor_tensor(a2.ap, a2.ap, lru_g[j], ALU.mult), [h, ready["g", j]])
                r_.free = i_.free = [h]
                lru.used = [y, last_ps, ix]
                a2.free = split(a2.ap, y, lru, j)

            rate[0] = 0
            gemm("mixb", DT, pairs(0, MH), inp, evict_q(mq, "mq"))
            gemm("mixb", DT, pairs(0, 2), inp, evict_q(dq, "dq"))
            for n in range(MH * TT + 2):
                def mem_slot(n=n):
                    if n < MH * TT:
                        mem_scores(n)
                    if n >= 2:
                        mem_values(n - 2)
                    if 0 <= n - 1 < MH * TT:
                        turn_first(n - 1, 2)
                filler.append(mem_slot)
            rate[0] = 1
            gemm("mixb", DT, pairs(2, 4), inp, evict_q(dq, "dq"))
            gemm("mixb", DT, pairs(0, 6), inp, evict_q(dk, "dk"))
            for g in range(3):
                gemm("mixb", DT, [[0, 1]], inp, evict_dv(g), rows=tok_tiles if g == 0 else res_tiles)
            flush()
            drain()
            for n in range(GH * DIL + 2):
                def values_and_scores(n=n):
                    if n >= 2:
                        dil_values(n - 2)
                    if n < GH * DIL:
                        dil_scores(n)
                filler.append(values_and_scores)
                if 0 <= n - 1 < GH * DIL:
                    filler.append(lambda n=n: turn_first(n - 1, 4))
                    filler.append(lambda n=n: turn_rest(n - 1))
            rate[0] = 4.5
            gemm("mixb", DT, [[j, 100 + j] for j in range(RT)], inp, evict_lru)
            flush()
            late_hooks.popleft()()
            drain()
            rate[0] = 1
            memo.used = [state["last"]]
            for h in range(MH):
                split(mq[h], ready["mo", h], memo, h)

            def evict_gate(branch, dst):
                def evict(j, ps, done):
                    t = tmp.take()
                    a = times_rstd(t.ap, ps, done, t.free)
                    hb = halfb[:, branch * DT + j:branch * DT + j + 1]
                    ready["th", j] = act.do(lambda e: e.activation(dst[j], t.ap, ACT.Tanh, bias=hb, scale=0.5),
                                            [a, fixed["half"], ready.get(("merged", j))])
                    t.free = [ready["th", j]]
                    return a
                return evict

            def evict_branch(order, dst):
                def evict(j, ps, done):
                    y = dve.do(lambda e: e.scalar_tensor_tensor(dst[j], dst[j], 1.0, ps, ALU.add, ALU.mult),
                               [done, ready["th", j]])
                    if order:
                        y2 = pool.do(lambda e: e.tensor_tensor(acc[j], acc[j], dst[j], ALU.add),
                                     [y, ready["acc", j]])
                        ready["merged", j] = ready["acc", j] = y2
                        if order == 2:
                            split(acc[j], y2, mrg, j)
                    else:
                        ready["acc", j] = y
                    return y
                return evict

            for order, (branch, name, n_k, src, dst) in enumerate((
                    (BRANCHES[0], "mem_out", MH, memo, acc), (BRANCHES[1], "lru_out", RT, lru, gate2),
                    (BRANCHES[2], "dil_out", 2, dil, gate2))):
                for j in range(0, DT, 2):
                    gemm("mixb", DT, [[j, j + 1]], inp, evict_gate(branch, dst))
                    gemm(name, n_k, [[j, j + 1]], src, evict_branch(order, dst))

            def evict_out(j, ps, done):
                step = add_residual(j, ps, done, 0.5)
                norm_tile(j, "g_mlp_2", ssum)
                return step
            gemm("out_b", DT, pairs(0, DT), mrg, evict_out)

        gained = Buf(m["gained_ssum"][:])
        final_rstd = Buf(m["final_rstd"][:])

        def final_tile(j):
            if j == 0:
                inp.ready = {}
            x = xT[j]
            x.free = [split(x.ap, x.ready, inp, j, scale=both_gains[:, j:j + 1], scale_ready=fixed["gains"]),
                      square_sum(x.ap, x.ready, j, ssum),
                      square_sum(x.ap, x.ready, j, gained, scale=col("norm_final", j))]

        def final_stats():
            sel_tiles = tok_tiles + res_tiles
            n = len(sel_tiles)
            for k, sums in enumerate((ssum, gained)):
                for i, tile in enumerate(sel_tiles):
                    got = pe.do(lambda e, at=k * n + i, tile=tile, sums=sums: e.matmul(
                        turn.ap[:, at:at + 1], tile(sums.ap), ones[:, 0:1], start=True, stop=True,
                        skip_group_check=True), [sums.ready, ones_set, turn.free])
                sums.free = [got]
            rsqrt(turn.ap[:, 0:n], got, n, D, hcol)
            turn.ready = [got]

        def final_product():
            n = TT + DIL
            r, v = hcol.ap[:, 0:n], stat_sb[:, 7, 0:n]
            a = dve.do(lambda e: e.tensor_tensor(v, r, r, ALU.mult), hcol.ready)
            b = dve.do(lambda e: e.tensor_tensor(v, v, turn.ap[:, n:2 * n], ALU.mult), [a, turn.ready])
            turn.free = [b]
            rsqrt(v, b, n, D, rcol)
            rcol.ready = [dve.do(lambda e: e.tensor_tensor(rcol.ap[:, 0:n], rcol.ap[:, 0:n], r, ALU.mult),
                                 rcol.ready)]

        def squares_only(j):
            xT[j].free = [square_sum(xT[j].ap, xT[j].ready, j, ssum)]

        def program():
            for l in range(DEPTH):
                norm_hooks(ssum, rcol, rstd)
                if l == 0:
                    hooks.extend([lambda g=g: bias_by_distance(g) for g in range(3)] + [small_constants])
                feed_forward(f"ffn1_in{l}", f"ffn1_out{l}", FF // P, True, 0.5,
                             lambda j, l=l: norm_tile(j, "norm_mix", ssum, DT * l))
                if l == 0:
                    lay_bias_rows()
                mixing1(l)
                norm_hooks(ssum, rcol, rstd)
                if l + 1 == DEPTH:
                    prepare_memory(region_free)
                feed_forward(f"ffn2_in{l}", f"ffn2_out{l}", FF // P, True, 0.5,
                             (lambda j, l=l: norm_tile(j, "norm_ffn1", ssum, DT * (l + 1))) if l + 1 < DEPTH
                             else final_tile)
            final_rstd.free = [memp.ready[j] for j in range(DT)]
            hooks.extend([lambda: None, lambda: None, final_stats, final_product,
                          lambda: (spread(rcol, rstd), spread(hcol, final_rstd))])
            hooks.extend([lambda j=j: [apply_norm(i, "norm_final", final_rstd) for i in (j, j + 1)]
                          for j in range(0, DT, 2)])
            memory_keys()
            memory_values()
            mixing2()
            norm_hooks(ssum, rcol, rstd)
            feed_forward("mlp_in", "mlp_out", FF2 // P, False, 1.0, squares_only)
            flush()
            stats(ssum, rcol, tok_tiles)
            spread(rcol, rstd)
            for j in range(DT):
                apply_norm(j, "g_final_2", rstd)

        Units.load_places += first_places
        for i in range(AHEAD):
            Units.places.append((act.place(), dve.place()))
            for j in range(i * DT // AHEAD, (i + 1) * DT // AHEAD):
                norm_tile(j, "norm_ffn1", ssum)
        mask_parts.extend([act.do(lambda e: e.activation(ident_r[:], ident[:], ACT.Copy), const_loads),
                           act.do(lambda e: e.activation(tri_r[:], tri[:], ACT.Copy), const_loads)])
        load_bias_tables()
        program()
        flush()
        stores = [load(out[:, j, :], xT[j].ap, out_sem, [xT[j].ready]) for j in range(DT)]

        count(lanes)
        stored = stores[-1].value
        block = ctx.enter_context(nc.Block())

        @block.sync
        def _(eng):
            emit(sp, eng)
            eng.wait_ge(out_sem, stored)

        @block.gpsimd
        def _(eng):
            emit(pool, eng)

        @block.scalar
        def _(eng):
            emit(act, eng)

        @block.vector
        def _(eng):
            emit(dve, eng)

        @block.tensor
        def _(eng):
            emit(pe, eng)


RET, FOX = RH * P, FH * FDH
MIX_AT = dict(rq=0, rk=RET, rv=2 * RET, rg=3 * RET, fq=4 * RET, fk=4 * RET + FOX, fv=4 * RET + 2 * FOX,
              ff=4 * RET + 3 * FOX, gates=4 * RET + 3 * FOX + FH)


QKV = 3 * GH * GD
MIX2_AT = dict(x=0, g=RNN, dq=2 * RNN, dk=2 * RNN + QKV, dv=2 * RNN + 2 * QKV, mq=2 * RNN + 3 * QKV,
               gates=2 * RNN + 3 * QKV + MH * P)


def starts(first_col, groups):
    return [[first_col + t * P for t in g] for g in groups]


def plans():
    out = {}
    for l in range(DEPTH):
        for k in (1, 2):
            pieces = ffn_pieces(FF // P)
            out[f"ffn{k}_in{l}"] = (f"w_ffn{k}_in", l, [(0, DT, starts(0, swiglu_groups(a, n))) for a, n in pieces])
            out[f"ffn{k}_out{l}"] = (f"w_ffn{k}_out", l, [(a, n, starts(0, pairs(0, DT))) for a, n in pieces])
        c = MIX_AT
        four = pairs(0, 4)
        out[f"mix{l}"] = ("w_in", l, [(0, DT, starts(c["fq"], four) + [[c["ff"]]] + starts(c["fk"], four)
                                       + starts(c["fv"], four) + starts(c["rq"], four) + starts(c["rk"], four)
                                       + starts(c["rv"], four) + starts(c["rg"], four)
                                       + starts(c["gates"], pairs(0, 2 * DT)))])
        out[f"w_o_ret{l}"] = ("w_o_ret", l, [(0, RH, starts(0, pairs(0, DT)))])
        out[f"w_o_fox{l}"] = ("w_o_fox", l, [(0, 4, starts(0, pairs(0, DT)))])
        out[f"w_out{l}"] = ("w_out", l, [(0, DT, starts(0, pairs(0, DT)))])
    c = MIX2_AT
    mem = pairs(0, MH)
    out["mem"] = ("w_mem_kv_2", None, [(0, DT, starts(0, mem) + starts(MH * P, mem))])
    mix = starts(c["mq"], mem) + starts(c["dq"], pairs(0, 6)) + starts(c["dk"], pairs(0, 6))
    mix += starts(c["dv"], pairs(0, 6)) + [[c["x"] + j * P, c["g"] + j * P] for j in range(RT)]
    for branch in BRANCHES:
        mix += starts(c["gates"] + branch * D, pairs(0, DT))
    out["mixb"] = ("w_in_2", None, [(0, DT, mix)])
    for name, src, n_k in (("lru_out", "w_lru_out_2", RT), ("dil_out", "w_dil_out_2", 2),
                           ("mem_out", "w_mem_out_2", MH), ("out_b", "w_out_2", DT)):
        out[name] = (src, None, [(0, n_k, starts(0, pairs(0, DT)))])
    out["mlp_in"] = ("w_mlp_in_2", None, [(0, DT, starts(0, pairs(a, n))) for a, n in ffn_pieces(FF2 // P)])
    out["mlp_out"] = ("w_mlp_out_2", None, [(a, n, starts(0, pairs(0, DT))) for a, n in ffn_pieces(FF2 // P)])
    return out


def pack(w, plan, ff_at=None):
    parts = []
    for k0, nk, groups in plan:
        for g in groups:
            for k, n in unit_blocks(nk, len(g)):
                rows = w[(k0 + k) * P:(k0 + k + n) * P].reshape(n, P, -1)
                cols = []
                for c in g:
                    if c == ff_at:
                        cols.append(np.concatenate([rows[:, :, c:c + FH], np.zeros((n, P, P - FH), w.dtype)], 2))
                    else:
                        cols.append(rows[:, :, c:c + P])
                parts.append(np.concatenate(cols, 2).transpose(1, 0, 2).reshape(-1))
    return np.concatenate(parts)


def constants():
    f = np.float32
    q, k = np.arange(P)[:, None], np.arange(P)[None, :]
    tri = np.where(k <= q, 0.0, NEG).astype(f)
    s_, t = np.arange(P)[:, None], np.arange(S)[None, :]
    gamma = 1.0 - 2.0 ** (-5.0 - np.arange(RH))
    decay = np.stack([np.where(t >= s_, g ** np.maximum(t - s_, 0).astype(np.float64), 0.0) for g in gamma], 1)
    half = P // 2
    inv = np.power(f(10000.0), -np.arange(0, P, 2, dtype=f) / f(P)).astype(f)
    ang = (np.arange(S, dtype=f)[None, :] * inv[:, None]).astype(f)
    cos, sin = np.cos(ang), np.sin(ang)
    cos2, sin2 = np.concatenate([cos, cos]), np.concatenate([-sin, sin])
    rope = np.stack([cos2, sin2, cos2 * f(P ** -0.5), sin2 * f(P ** -0.5)], 1)
    sel = np.zeros((PARTS, FH, P), f)
    sel[np.arange(FH), np.arange(FH)] = sel[32 + np.arange(FH), np.arange(FH)] = 1.0
    y = np.arange(2 * S) - (S - 1)
    onehot, band = np.zeros((NB, 3, 2 * S), f), np.full((3, 2 * S), NEG, f)
    for g, dist in enumerate((-y, -4 * y, np.where(y % 4 == 0, -4 * y, -1))):
        ok = (dist >= 0) & (dist <= (P, 4 * P, 16 * P)[g]) & (y > -P - (g == 0))
        near = np.maximum(dist, 1).astype(f)
        large = NB // 2 + (np.log(near / f(NB // 2)) / f(np.log(2048 / (NB // 2))) * f(NB // 2)).astype(np.int32)
        bucket = np.where(dist < NB // 2, dist, np.minimum(large, NB - 1))
        onehot[bucket[ok], g, np.nonzero(ok)[0]] = 1.0
        band[g, ok] = 0.0
    band = np.broadcast_to(band, (GH, 3, 2 * S)).copy()
    return dict(onehot_in=onehot, band_in=band, ident_in=np.eye(P, dtype=f), tri_in=tri,
                decay_in=decay.astype(f), rope_in=rope.astype(f), sel_in=sel.reshape(PARTS, FH * P))


def columns(a):
    return a.reshape(-1, P).T


def small_vectors(x):
    parts = []
    for name, (_, n) in VEC.items():
        a = np.asarray(x[name])
        if name == "b_forget":
            c = np.zeros((P, n), a.dtype)
            c[:FH] = a.T
        else:
            c = columns(a.reshape(-1))
        parts.append(c)
    return np.ascontiguousarray(np.concatenate(parts, 1))


def arrays_of(inputs):
    f = {k: np.asarray(v) for k, v in inputs.items()}
    arrays = dict(constants())
    arrays["x_in"] = np.ascontiguousarray(f["x"][0].T.reshape(DT, P, S).transpose(1, 0, 2))
    arrays["vec_in"] = small_vectors(f)
    arrays["mem_in"] = np.ascontiguousarray(f["mem_2"][0].T.reshape(DT, P, NMEM).transpose(1, 0, 2))
    arrays["table_in"] = np.ascontiguousarray(f["rel_bias_2"])
    rg = np.zeros((RT, P, 2, P), np.float32)
    for k, name in enumerate(("w_rg_a_2", "w_rg_x_2")):
        for b in range(2):
            rg[:, b * 64:b * 64 + 64, k, b * 64:b * 64 + 64] = f[name][b::2]
    arrays["rg_in"] = rg.reshape(RT, P, 2 * P)
    for name, (src, l, plan) in plans().items():
        w = f[src] if l is None else f[src][l]
        arrays["w_" + name] = pack(w, plan, MIX_AT["ff"] if src == "w_in" else None)
    return arrays


ORDER = ["x_in", "vec_in", "ident_in", "tri_in", "decay_in", "rope_in", "sel_in", "mem_in", "onehot_in", "band_in",
         "table_in", "rg_in"]


def kernel(**inputs):
    import concourse.bacc as bacc
    from concourse.bass_utils import run_bass_kernel_spmd

    nc = bacc.Bacc("TRN2", target_bir_lowering=False, num_devices=1)
    arrays = arrays_of(inputs)
    aps = {name: nc.dram_tensor(name, a.shape, mybir.dt.from_np(a.dtype), kind="ExternalInput").ap()
           for name, a in arrays.items()}
    out = nc.dram_tensor("out", (P, DT, S), F32, kind="ExternalOutput").ap()
    w = {name[2:]: ap for name, ap in aps.items() if name.startswith("w_")}
    build(nc, *[aps[name] for name in ORDER], w, out)
    r = run_bass_kernel_spmd(nc, [arrays], core_ids=[0])
    y = r.results[0]["out"]
    return y.transpose(1, 0, 2).reshape(D, S).T.reshape(1, S, D)
```
